# Optimizing a Trainium2 kernel written in Bass

```python
import jax, jax.numpy as jnp
from jax import lax
import numpy as np
import math

D_MODEL = 1024
BATCH = 1
SEQ = 256
DEPTH = 1

CTX_LEN = 256
GRID_W = 64
D_MIX = 1024
HEAD_DIM = 64
N_Q_HEADS = 8
N_KV_HEADS = 2
Q_PER_KV = N_Q_HEADS // N_KV_HEADS
D_ATTN = N_Q_HEADS * HEAD_DIM
D_KV = N_KV_HEADS * HEAD_DIM
N_GM_GROUPS = 8
GM_GROUP_DIM = 64
D_GM = N_GM_GROUPS * GM_GROUP_DIM
CHUNK = 128
Q_BLOCK = 128
D_IN = D_ATTN + 2 * D_KV + 2 * D_GM
ROPE_THETA = 10000.0
N_EXPERTS = 16
CAPACITY_FACTOR = 2
EXPERT_FF = 2048
EPS = 1e-6


def rmsnorm(x, g):
    xf = x.astype(jnp.float32)
    y = xf * lax.rsqrt(jnp.mean(xf * xf, axis=-1, keepdims=True) + EPS)
    return (y * g.astype(jnp.float32)).astype(x.dtype)

def adaln(cvec, w_mod, b_mod):
    m = jax.nn.silu(cvec) @ w_mod + b_mod
    return jnp.split(m, 6, axis=-1)

def axial_rope(row, col):
    n_freq = HEAD_DIM // 4
    inv = ROPE_THETA ** (-jnp.arange(n_freq, dtype=jnp.float32) / n_freq)
    ang = jnp.concatenate([row[:, None].astype(jnp.float32) * inv,
                           col[:, None].astype(jnp.float32) * inv], axis=-1)
    return jnp.cos(ang), jnp.sin(ang)

def apply_rope(x, cos, sin):
    shape = (cos.shape[0],) + (1,) * (x.ndim - 3) + (cos.shape[-1],)
    cos = cos.reshape(shape).astype(x.dtype)
    sin = sin.reshape(shape).astype(x.dtype)
    x1, x2 = jnp.split(x, 2, axis=-1)
    return jnp.concatenate([x1 * cos - x2 * sin, x1 * sin + x2 * cos], axis=-1)

def modulate(x, g, shift, scale):
    return rmsnorm(x, g) * (1 + scale) + shift

def split_in_proj(w_in):
    return jnp.split(w_in, [D_ATTN, D_ATTN + 2 * D_KV], axis=1)

def queries(h, w_q, q_gain):
    b, n = h.shape[:2]
    return rmsnorm((h @ w_q).reshape(b, n, N_KV_HEADS, Q_PER_KV, HEAD_DIM), q_gain)

def keys_values(h, w_kv, k_gain):
    b, n = h.shape[:2]
    k, v = jnp.split(h @ w_kv, 2, axis=-1)
    k = rmsnorm(k.reshape(b, n, N_KV_HEADS, HEAD_DIM), k_gain)
    return k, v.reshape(b, n, N_KV_HEADS, HEAD_DIM)

def gqa_attend(q, k, v):
    b, nq = q.shape[:2]
    scale = HEAD_DIM ** -0.5

    def block(qb):
        s = jnp.einsum('bqkgd,bskd->bkgqs', qb, k).astype(jnp.float32) * scale
        p = jax.nn.softmax(s, axis=-1).astype(v.dtype)
        return jnp.einsum('bkgqs,bskd->bqkgd', p, v)

    nb = nq // Q_BLOCK
    qb = jnp.moveaxis(q.reshape(b, nb, Q_BLOCK, N_KV_HEADS, Q_PER_KV, HEAD_DIM), 1, 0)
    o = lax.map(block, qb)
    return jnp.moveaxis(o, 0, 1).reshape(b, nq, D_ATTN)

def spatial_gating(h, w_gm, v_gain, w_s, b_s):
    b, n = h.shape[:2]
    u, vv = jnp.split(jax.nn.gelu(h @ w_gm, approximate=False), 2, axis=-1)
    vv = rmsnorm(vv, v_gain).reshape(b, n // CHUNK, CHUNK, N_GM_GROUPS, GM_GROUP_DIM)
    mixed = jnp.einsum('gij,bcjgd->bcigd', w_s, vv) + b_s.T[:, :, None]
    return u * mixed.reshape(b, n, D_GM)

def expert_choice_ffn(h, w_router, w1, w3, w2):
    n, d = h.shape[1], h.shape[2]
    cap = CAPACITY_FACTOR * n // N_EXPERTS
    aff = jax.nn.softmax((h @ w_router).astype(jnp.float32), axis=-1)
    gate, idx = lax.top_k(jnp.swapaxes(aff, 1, 2), cap)
    xe = jax.vmap(lambda hb, ib: hb[ib])(h, idx)
    hid = jax.nn.silu(jnp.einsum('becd,edf->becf', xe, w1)) * jnp.einsum('becd,edf->becf', xe, w3)
    ye = jnp.einsum('becf,efd->becd', hid, w2) * gate[..., None].astype(h.dtype)

    def scatter(yb, ib):
        return jnp.zeros((n, d), h.dtype).at[ib.reshape(-1)].add(yb.reshape(-1, d))

    return jax.vmap(scatter)(ye, idx)

def hybrid_layer(xl, xc, c, c_ctx, cos, sin, w_mod, b_mod, g_mix, g_ffn, w_in, q_gain, k_gain,
                 v_gain, w_s, b_s, w_out, w_router, w1, w3, w2, update_ctx):
    sh1, sc1, gt1, sh2, sc2, gt2 = [m[:, None, :] for m in adaln(c, w_mod, b_mod)]
    csh1, csc1, cgt1, csh2, csc2, cgt2 = adaln(c_ctx, w_mod, b_mod)
    w_q, w_kv, w_gm = split_in_proj(w_in)

    hl = modulate(xl, g_mix, sh1, sc1)
    hc = modulate(xc, g_mix, csh1, csc1)
    kc, vc = keys_values(hc, w_kv, k_gain)
    ql = apply_rope(queries(hl, w_q, q_gain), cos, sin)
    kl, vl = keys_values(hl, w_kv, k_gain)
    kl = apply_rope(kl, cos, sin)
    k_all = jnp.concatenate([kl, kc], axis=1)
    v_all = jnp.concatenate([vl, vc], axis=1)
    mix_l = jnp.concatenate([gqa_attend(ql, k_all, v_all),
                             spatial_gating(hl, w_gm, v_gain, w_s, b_s)], axis=-1)
    xl_new = xl + gt1 * (mix_l @ w_out)

    xl_new = xl_new + gt2 * expert_choice_ffn(modulate(xl_new, g_ffn, sh2, sc2), w_router, w1, w3, w2)

    if update_ctx:
        qc = queries(hc, w_q, q_gain)
        mix_c = jnp.concatenate([gqa_attend(qc, kc, vc),
                                 spatial_gating(hc, w_gm, v_gain, w_s, b_s)], axis=-1)
        xc = xc + cgt1 * (mix_c @ w_out)
        xc = xc + cgt2 * expert_choice_ffn(modulate(xc, g_ffn, csh2, csc2), w_router, w1, w3, w2)
    return xl_new, xc

def first_inputs(seed: int = 0) -> dict:
    key = jax.random.key(seed)
    ks = jax.random.split(key, 21)
    f32 = jnp.float32
    L = DEPTH

    def nrm(k, shape, s):
        return jax.random.normal(k, shape, f32) * s

    return {
        "x": nrm(ks[0], (BATCH, SEQ, D_MODEL), 1.0),
        "c": nrm(ks[1], (BATCH, D_MODEL), 1.0),
        "ctx": nrm(ks[2], (BATCH, CTX_LEN, D_MODEL), 1.0),
        "c_ctx": nrm(ks[3], (D_MODEL,), 1.0),
        "w_mod": nrm(ks[4], (L, D_MODEL, 6 * D_MODEL), D_MODEL ** -0.5),
        "b_mod": nrm(ks[5], (L, 6 * D_MODEL), 0.02),
        "g_mix": 1.0 + nrm(ks[6], (L, D_MODEL), 0.02),
        "g_ffn": 1.0 + nrm(ks[7], (L, D_MODEL), 0.02),
        "w_in": nrm(ks[8], (L, D_MODEL, D_IN), D_MODEL ** -0.5),
        "q_gain": 1.0 + nrm(ks[9], (L, HEAD_DIM), 0.02),
        "k_gain": 1.0 + nrm(ks[10], (L, HEAD_DIM), 0.02),
        "v_gain": 1.0 + nrm(ks[11], (L, D_GM), 0.02),
        "w_s": nrm(ks[12], (L, N_GM_GROUPS, CHUNK, CHUNK), CHUNK ** -0.5),
        "b_s": 1.0 + nrm(ks[13], (L, N_GM_GROUPS, CHUNK), 0.02),
        "w_out": nrm(ks[14], (L, D_MIX, D_MODEL), D_MIX ** -0.5),
        "w_router": nrm(ks[15], (L, D_MODEL, N_EXPERTS), D_MODEL ** -0.5),
        "w1": nrm(ks[16], (L, N_EXPERTS, D_MODEL, EXPERT_FF), D_MODEL ** -0.5),
        "w3": nrm(ks[17], (L, N_EXPERTS, D_MODEL, EXPERT_FF), D_MODEL ** -0.5),
        "w2": nrm(ks[18], (L, N_EXPERTS, EXPERT_FF, D_MODEL), EXPERT_FF ** -0.5),
        "g_final": 1.0 + nrm(ks[19], (D_MODEL,), 0.02),
    }

def first_block(x, c, ctx, c_ctx, w_mod, b_mod, g_mix, g_ffn, w_in, q_gain, k_gain, v_gain,
              w_s, b_s, w_out, w_router, w1, w3, w2, g_final):
    n_lat = x.shape[1]
    rows = n_lat // GRID_W
    row = jnp.repeat(jnp.arange(rows), GRID_W)
    col = jnp.tile(jnp.arange(GRID_W), rows)
    cos, sin = axial_rope(row, col)
    xl, xc = x, ctx
    for layer in range(DEPTH):
        xl, xc = hybrid_layer(xl, xc, c, c_ctx, cos, sin, w_mod[layer], b_mod[layer], g_mix[layer],
                              g_ffn[layer], w_in[layer], q_gain[layer], k_gain[layer], v_gain[layer],
                              w_s[layer], b_s[layer], w_out[layer], w_router[layer], w1[layer],
                              w3[layer], w2[layer], update_ctx=layer + 1 < DEPTH)
    return rmsnorm(xl, g_final)


DEPTH_2 = 2

MIX_W = 512
N_BRANCH = 4
SWA_HEADS = 8
SWA_KV_HEADS = 2
SWA_WINDOW = 128
CONV_K = 3
NSA_HEADS = 8
NSA_KV_HEADS = 2
CMP_BLOCK = 32
CMP_STRIDE = 16
CMP_HIDDEN = 256
SEL_BLOCK = 64
SEL_TOPK = 16
NSA_WINDOW = 512
RET_HEADS = 4
RET_QK_DIM = 64
RET_V_DIM = 128
RET_CHUNK = 128
ROPE_BASE = 10000.0
D_FF = 2816

SWA_Q = SWA_HEADS * HEAD_DIM
SWA_KV = SWA_KV_HEADS * HEAD_DIM
NSA_Q = NSA_HEADS * HEAD_DIM
NSA_KV = NSA_KV_HEADS * HEAD_DIM
RET_QK = RET_HEADS * RET_QK_DIM
RET_V = RET_HEADS * RET_V_DIM
IN_WIDTHS = (
    SWA_Q, SWA_KV, SWA_KV,
    MIX_W, MIX_W, MIX_W,
    NSA_Q, NSA_KV, NSA_KV, NSA_KV, NSA_KV, NSA_KV, NSA_KV,
    NSA_HEADS * 3,
    RET_QK, RET_QK, RET_V, RET_V,
    N_BRANCH * D_MODEL,
)
IN_TOTAL = sum(IN_WIDTHS)
SPLIT_POINTS = tuple(int(v) for v in np.cumsum(IN_WIDTHS)[:-1])


def rms_norm(x, g):
    xf = x.astype(jnp.float32)
    y = xf * lax.rsqrt(jnp.mean(xf * xf, axis=-1, keepdims=True) + EPS)
    return (y * g.astype(jnp.float32)).astype(x.dtype)

def heads(t, n):
    b, s, _ = t.shape
    return t.reshape(b, s, n, -1).transpose(0, 2, 1, 3)

def merge_heads(t):
    b, n, s, d = t.shape
    return t.transpose(0, 2, 1, 3).reshape(b, s, n * d)

def swiglu(x, w_gate, w_up, w_down):
    return (jax.nn.silu(x @ w_gate) * (x @ w_up)) @ w_down

def masked_softmax(s, mask, sink=None):
    s = jnp.where(mask, s.astype(jnp.float32), -jnp.inf)
    m = jnp.max(s, axis=-1, keepdims=True)
    if sink is not None:
        m = jnp.maximum(m, sink)
    m = jnp.where(jnp.isfinite(m), m, 0.0)
    p = jnp.exp(s - m)
    denom = jnp.sum(p, axis=-1, keepdims=True)
    if sink is not None:
        denom = denom + jnp.exp(sink - m)
    return p / jnp.maximum(denom, 1e-30)

def banded_attention(q, k, v, window, sink=None):
    b, h, t, d = q.shape
    g = k.shape[1]
    r = h // g
    n_blk = t // Q_BLOCK
    pad = window
    span = pad + Q_BLOCK
    kp = jnp.pad(k, ((0, 0), (0, 0), (pad, 0), (0, 0)))
    vp = jnp.pad(v, ((0, 0), (0, 0), (pad, 0), (0, 0)))
    qb = q.reshape(b, g, r, n_blk, Q_BLOCK, d).transpose(3, 0, 1, 2, 4, 5)
    scale = d ** -0.5

    def one_block(args):
        qi, i = args
        start = i * Q_BLOCK
        ki = lax.dynamic_slice_in_dim(kp, start, span, axis=2)
        vi = lax.dynamic_slice_in_dim(vp, start, span, axis=2)
        qpos = start + jnp.arange(Q_BLOCK)
        kpos = start - pad + jnp.arange(span)
        diff = qpos[:, None] - kpos[None, :]
        mask = (kpos[None, :] >= 0) & (diff >= 0) & (diff < window)
        s = jnp.einsum('bgrqd,bgkd->bgrqk', qi, ki) * scale
        p = masked_softmax(s, mask, sink)
        return jnp.einsum('bgrqk,bgkd->bgrqd', p.astype(vi.dtype), vi)

    out = lax.map(one_block, (qb, jnp.arange(n_blk)))
    return out.transpose(1, 2, 3, 0, 4, 5).reshape(b, h, t, d)

def swa_sink_mixer(q, k, v, q_gain, k_gain, sinks):
    q = rms_norm(heads(q, SWA_HEADS), q_gain)
    k = rms_norm(heads(k, SWA_KV_HEADS), k_gain)
    v = heads(v, SWA_KV_HEADS)
    sink = sinks.astype(jnp.float32).reshape(1, SWA_KV_HEADS, SWA_HEADS // SWA_KV_HEADS, 1, 1)
    return merge_heads(banded_attention(q, k, v, SWA_WINDOW, sink))

def short_conv_mixer(x_in, gate_b, gate_c, conv_w):
    z = gate_c * x_in
    y = lax.conv_general_dilated(z, conv_w.astype(z.dtype), window_strides=(1,),
                                 padding=((CONV_K - 1, 0),),
                                 dimension_numbers=('NWC', 'WIO', 'NWC'),
                                 feature_group_count=z.shape[-1])
    return gate_b * y

def nsa_mixer(q, kc, vc, ks, vs, kw, vw, gate_logits, q_gain, k_gain,
              pos_k, pos_v, wk1, wk2, wv1, wv2):
    b, t, _ = q.shape
    g = NSA_KV_HEADS
    r = NSA_HEADS // g
    d = HEAD_DIM
    q = rms_norm(heads(q, NSA_HEADS), q_gain)

    kw = rms_norm(heads(kw, g), k_gain[2])
    o_win = banded_attention(q, kw, heads(vw, g), NSA_WINDOW)

    n_cmp = (t - CMP_BLOCK) // CMP_STRIDE + 1
    cmp_start = jnp.arange(n_cmp) * CMP_STRIDE
    cmp_end = cmp_start + CMP_BLOCK - 1
    idx = cmp_start[:, None] + jnp.arange(CMP_BLOCK)[None, :]

    def compress(tok, pe, w1, w2):
        blk = heads(tok, g)[:, :, idx] + pe
        blk = blk.reshape(b, g, n_cmp, CMP_BLOCK * d)
        return jax.nn.gelu(blk @ w1) @ w2

    k_cmp = rms_norm(compress(kc, pos_k, wk1, wk2), k_gain[0])
    v_cmp = compress(vc, pos_v, wv1, wv2)

    n_sel = t // SEL_BLOCK
    sel_k = min(SEL_TOPK, n_sel)
    ks_blk = rms_norm(heads(ks, g), k_gain[1]).reshape(b, g, n_sel, SEL_BLOCK, d)
    vs_blk = heads(vs, g).reshape(b, g, n_sel, SEL_BLOCK, d)
    sel_start = jnp.arange(n_sel) * SEL_BLOCK
    overlap = ((cmp_start[:, None] < sel_start[None, :] + SEL_BLOCK)
               & (cmp_end[:, None] >= sel_start[None, :])).astype(jnp.float32)
    blk_id = jnp.arange(n_sel)
    bi = jnp.arange(b)[:, None, None, None]
    gi = jnp.arange(g)[None, :, None, None]

    n_blk = t // Q_BLOCK
    qb = q.reshape(b, g, r, n_blk, Q_BLOCK, d).transpose(3, 0, 1, 2, 4, 5)
    scale = d ** -0.5

    def one_block(args):
        qi, i = args
        qpos = i * Q_BLOCK + jnp.arange(Q_BLOCK)
        s = jnp.einsum('bgrqd,bgnd->bgrqn', qi, k_cmp) * scale
        p_cmp = masked_softmax(s, cmp_end[None, :] <= qpos[:, None])
        o_cmp = jnp.einsum('bgrqn,bgnd->bgrqd', p_cmp.astype(qi.dtype), v_cmp)
        imp = jnp.einsum('bgrqn,ns->bgqs', p_cmp, overlap)
        cur = qpos // SEL_BLOCK
        causal = blk_id[None, :] <= cur[:, None]
        forced = ((blk_id[None, :] == 0) | (blk_id[None, :] == cur[:, None])
                  | (blk_id[None, :] == cur[:, None] - 1))
        imp = jnp.where(forced, jnp.inf, imp)
        imp = jnp.where(causal, imp, -jnp.inf)
        top_s, top_i = lax.top_k(imp, sel_k)
        valid = top_s > -jnp.inf
        k_g = ks_blk[bi, gi, top_i]
        v_g = vs_blk[bi, gi, top_i]
        tok_pos = top_i[..., None] * SEL_BLOCK + jnp.arange(SEL_BLOCK)
        mask = valid[..., None] & (tok_pos <= qpos[:, None, None])
        mask = mask.reshape(b, g, 1, Q_BLOCK, sel_k * SEL_BLOCK)
        s = jnp.einsum('bgrqd,bgqkld->bgrqkl', qi, k_g) * scale
        s = s.reshape(b, g, r, Q_BLOCK, sel_k * SEL_BLOCK)
        p = masked_softmax(s, mask)
        v_g = v_g.reshape(b, g, Q_BLOCK, sel_k * SEL_BLOCK, d)
        o_sel = jnp.einsum('bgrqm,bgqmd->bgrqd', p.astype(v_g.dtype), v_g)
        return o_cmp, o_sel

    o_cmp, o_sel = lax.map(one_block, (qb, jnp.arange(n_blk)))
    o_cmp = o_cmp.transpose(1, 2, 3, 0, 4, 5).reshape(b, NSA_HEADS, t, d)
    o_sel = o_sel.transpose(1, 2, 3, 0, 4, 5).reshape(b, NSA_HEADS, t, d)
    gates = jax.nn.sigmoid(gate_logits.astype(jnp.float32)).astype(q.dtype)
    gates = gates.reshape(b, t, NSA_HEADS, 3).transpose(0, 2, 1, 3)
    o = gates[..., 0:1] * o_cmp + gates[..., 1:2] * o_sel + gates[..., 2:3] * o_win
    return merge_heads(o)

def rotary(x, pos):
    half = x.shape[-1] // 2
    inv = ROPE_BASE ** (-jnp.arange(half, dtype=jnp.float32) / half)
    ang = pos.astype(jnp.float32)[:, None] * inv[None, :]
    cos = jnp.cos(ang).astype(x.dtype)
    sin = jnp.sin(ang).astype(x.dtype)
    x1, x2 = x[..., :half], x[..., half:]
    return jnp.concatenate([x1 * cos - x2 * sin, x1 * sin + x2 * cos], axis=-1)

def retention_mixer(q, k, v, gate, norm_gain):
    b, t, _ = q.shape
    h, c = RET_HEADS, RET_CHUNK
    nc = t // c
    dt = q.dtype
    pos = jnp.arange(t)
    q = rotary(heads(q, h), pos)
    k = rotary(heads(k, h), pos) * (RET_QK_DIM ** -0.5)
    v = heads(v, h)
    log_gamma = jnp.log(1.0 - 2.0 ** (-5.0 - jnp.arange(h, dtype=jnp.float32)))
    j = jnp.arange(c, dtype=jnp.float32)
    diff = j[:, None] - j[None, :]
    dmask = jnp.where(diff >= 0, jnp.exp(diff * log_gamma[:, None, None]), 0.0)
    qc = q.reshape(b, h, nc, c, RET_QK_DIM)
    kc = k.reshape(b, h, nc, c, RET_QK_DIM)
    vc = v.reshape(b, h, nc, c, RET_V_DIM)
    att = jnp.einsum('bhncd,bhnmd->bhncm', qc, kc) * dmask[:, None].astype(dt)
    o = jnp.einsum('bhncm,bhnme->bhnce', att, vc)
    zeta = jnp.exp((c - 1 - j) * log_gamma[:, None]).astype(dt)
    s_chunk = jnp.einsum('bhnmd,bhnme->nbhde', kc * zeta[:, None, :, None], vc)
    decay_chunk = jnp.exp(c * log_gamma).astype(dt)[None, :, None, None]

    def step(r_prev, s_i):
        return r_prev * decay_chunk + s_i, r_prev

    _, r_before = lax.scan(step, jnp.zeros_like(s_chunk[0]), s_chunk)
    xi = jnp.exp((j + 1.0) * log_gamma[:, None]).astype(dt)
    o = o + jnp.einsum('bhncd,nbhde->bhnce', qc * xi[:, None, :, None], r_before)
    o = o.reshape(b, h, t, RET_V_DIM).astype(jnp.float32)
    mu = jnp.mean(o, axis=-1, keepdims=True)
    var = jnp.mean(jnp.square(o - mu), axis=-1, keepdims=True)
    o = ((o - mu) * lax.rsqrt(var + EPS)).astype(dt)
    o = merge_heads(o) * norm_gain
    return jax.nn.silu(gate) * o

def second_inputs(seed: int = 0) -> dict:
    key = jax.random.key(seed)
    ks = iter(jax.random.split(key, 40))
    f32 = jnp.float32

    def nrm(shape, scale):
        return jax.random.normal(next(ks), shape, f32) * scale

    def gain(shape):
        return 1.0 + 0.02 * jax.random.normal(next(ks), shape, f32)

    L, D = DEPTH_2, D_MODEL
    return {
        "x": jax.random.normal(next(ks), (BATCH, SEQ, D), f32),
        "ffn1_norm": gain((L, D)),
        "ffn1_w_gate": nrm((L, D, D_FF), D ** -0.5),
        "ffn1_w_up": nrm((L, D, D_FF), D ** -0.5),
        "ffn1_w_down": nrm((L, D_FF, D), D_FF ** -0.5),
        "mix_norm": gain((L, D)),
        "w_in": nrm((L, D, IN_TOTAL), D ** -0.5),
        "merge_gate_bias": nrm((L, N_BRANCH * D), 0.01),
        "swa_q_gain": gain((L, HEAD_DIM)),
        "swa_k_gain": gain((L, HEAD_DIM)),
        "swa_sinks": nrm((L, SWA_HEADS), 1.0),
        "conv_w": nrm((L, CONV_K, 1, MIX_W), CONV_K ** -0.5),
        "nsa_q_gain": gain((L, HEAD_DIM)),
        "nsa_k_gain": gain((L, 3, HEAD_DIM)),
        "cmp_pos_k": nrm((L, CMP_BLOCK, HEAD_DIM), 0.02),
        "cmp_pos_v": nrm((L, CMP_BLOCK, HEAD_DIM), 0.02),
        "cmp_wk1": nrm((L, CMP_BLOCK * HEAD_DIM, CMP_HIDDEN), (CMP_BLOCK * HEAD_DIM) ** -0.5),
        "cmp_wk2": nrm((L, CMP_HIDDEN, HEAD_DIM), CMP_HIDDEN ** -0.5),
        "cmp_wv1": nrm((L, CMP_BLOCK * HEAD_DIM, CMP_HIDDEN), (CMP_BLOCK * HEAD_DIM) ** -0.5),
        "cmp_wv2": nrm((L, CMP_HIDDEN, HEAD_DIM), CMP_HIDDEN ** -0.5),
        "ret_norm_gain": gain((L, RET_V)),
        "w_branch": nrm((L, N_BRANCH, MIX_W, D), MIX_W ** -0.5),
        "w_out": nrm((L, D, D), D ** -0.5),
        "ffn2_norm": gain((L, D)),
        "ffn2_w_gate": nrm((L, D, D_FF), D ** -0.5),
        "ffn2_w_up": nrm((L, D, D_FF), D ** -0.5),
        "ffn2_w_down": nrm((L, D_FF, D), D_FF ** -0.5),
    }

def second_block(x, ffn1_norm, ffn1_w_gate, ffn1_w_up, ffn1_w_down, mix_norm, w_in,
              merge_gate_bias, swa_q_gain, swa_k_gain, swa_sinks, conv_w, nsa_q_gain,
              nsa_k_gain, cmp_pos_k, cmp_pos_v, cmp_wk1, cmp_wk2, cmp_wv1, cmp_wv2,
              ret_norm_gain, w_branch, w_out, ffn2_norm, ffn2_w_gate, ffn2_w_up,
              ffn2_w_down):
    b, t, _ = x.shape
    for l in range(DEPTH_2):
        x = x + 0.5 * swiglu(rms_norm(x, ffn1_norm[l]), ffn1_w_gate[l], ffn1_w_up[l], ffn1_w_down[l])
        u = rms_norm(x, mix_norm[l])
        (a_q, a_k, a_v, b_x, b_b, b_c,
         c_q, c_kc, c_vc, c_ks, c_vs, c_kw, c_vw, c_g,
         d_q, d_k, d_v, d_g, gate_logits) = jnp.split(u @ w_in[l], SPLIT_POINTS, axis=-1)
        y_a = swa_sink_mixer(a_q, a_k, a_v, swa_q_gain[l], swa_k_gain[l], swa_sinks[l])
        y_b = short_conv_mixer(b_x, b_b, b_c, conv_w[l])
        y_c = nsa_mixer(c_q, c_kc, c_vc, c_ks, c_vs, c_kw, c_vw, c_g, nsa_q_gain[l],
                        nsa_k_gain[l], cmp_pos_k[l], cmp_pos_v[l], cmp_wk1[l], cmp_wk2[l],
                        cmp_wv1[l], cmp_wv2[l])
        y_d = retention_mixer(d_q, d_k, d_v, d_g, ret_norm_gain[l])
        ys = jnp.stack([y_a, y_b, y_c, y_d], axis=2)
        branch = jnp.einsum('btnw,nwd->btnd', ys, w_branch[l])
        gates = jax.nn.sigmoid((gate_logits + merge_gate_bias[l]).astype(jnp.float32))
        gates = gates.astype(x.dtype).reshape(b, t, N_BRANCH, D_MODEL)
        merged = jnp.sum(gates * branch, axis=2)
        x = x + merged @ w_out[l]
        x = x + 0.5 * swiglu(rms_norm(x, ffn2_norm[l]), ffn2_w_gate[l], ffn2_w_up[l], ffn2_w_down[l])
    return x


def setup_inputs(seed=0):
    out = dict(first_inputs(seed))
    for name, value in second_inputs(seed + 1).items():
        if name != "x":
            out[name + "_2"] = value
    return out


def reference(
    x, c, ctx, c_ctx, w_mod, b_mod, g_mix, g_ffn, w_in, q_gain, k_gain, v_gain, w_s, b_s, w_out,
    w_router, w1, w3, w2, g_final, ffn1_norm_2, ffn1_w_gate_2, ffn1_w_up_2, ffn1_w_down_2,
    mix_norm_2, w_in_2, merge_gate_bias_2, swa_q_gain_2, swa_k_gain_2, swa_sinks_2, conv_w_2,
    nsa_q_gain_2, nsa_k_gain_2, cmp_pos_k_2, cmp_pos_v_2, cmp_wk1_2, cmp_wk2_2, cmp_wv1_2,
    cmp_wv2_2, ret_norm_gain_2, w_branch_2, w_out_2, ffn2_norm_2, ffn2_w_gate_2, ffn2_w_up_2,
    ffn2_w_down_2,
):
    x = first_block(
        x, c, ctx, c_ctx, w_mod, b_mod, g_mix, g_ffn, w_in, q_gain, k_gain, v_gain, w_s, b_s,
        w_out, w_router, w1, w3, w2, g_final,
    )
    return second_block(
        x, ffn1_norm_2, ffn1_w_gate_2, ffn1_w_up_2, ffn1_w_down_2, mix_norm_2, w_in_2,
        merge_gate_bias_2, swa_q_gain_2, swa_k_gain_2, swa_sinks_2, conv_w_2, nsa_q_gain_2,
        nsa_k_gain_2, cmp_pos_k_2, cmp_pos_v_2, cmp_wk1_2, cmp_wk2_2, cmp_wv1_2, cmp_wv2_2,
        ret_norm_gain_2, w_branch_2, w_out_2, ffn2_norm_2, ffn2_w_gate_2, ffn2_w_up_2,
        ffn2_w_down_2,
    )


_drawn_inputs = setup_inputs


def setup_inputs(seed=0):
    import zlib

    import numpy as np

    out = dict(_drawn_inputs(seed))
    spreads = {}
    factors = {'q_gain': 8.0,
     'k_gain': 8.0,
     'ffn1_norm_2': 3.608,
     'merge_gate_bias_2': 8.0,
     'swa_q_gain_2': 23.153,
     'swa_k_gain_2': 80.776,
     'swa_sinks_2': 200.0,
     'nsa_q_gain_2': 67.173,
     'nsa_k_gain_2': 65.395,
     'cmp_pos_k_2': 24.534,
     'cmp_pos_v_2': 40.875,
     'ret_norm_gain_2': 23.028,
     'ffn2_norm_2': 5.539}
    for name, (base, spread) in spreads.items():
        noise = np.random.default_rng([zlib.crc32(name.encode()), seed]).standard_normal(out[name].shape)
        drawn = base * np.exp(spread * noise) if base else spread * noise
        out[name] = __import__('jax').numpy.asarray(drawn.astype(out[name].dtype))
    for name, factor in factors.items():
        out[name] = (out[name] * factor).astype(out[name].dtype)
    return out
```

```python
from contextlib import ExitStack

import concourse.bass as bass
import numpy as np
from concourse import mybir

ALU = mybir.AluOpType
ACT = mybir.ActivationFunctionType
F32 = mybir.dt.float32
U32 = mybir.dt.uint32
AX_X = mybir.AxisListType.X

P = 128
D = 1024
KC = D // P
T = 256
TT = T // P
HD = 64
EPS = 1e-6
SCALE = HD ** -0.5
NEG = -1e30
FLOOR = 1e25
TINY = 1e-30

NE = 16
CAP = 2 * T // NE
EFF = 2048
NL = 2
FF = 2816
FCH = FF // P
NCMP = (T - 32) // 16 + 1
IN2 = 9240

RING = 12
UNIT = 2048
U_MOD = 0
U_WIN = 24
U_WOUT = 31
U_ROUTER = 35
U_EXPERT = 36
EXPERT_UNITS = 24
U_LAYER = U_EXPERT + NE * EXPERT_UNITS
L_FFN1 = 0
L_TOK = 33
L_FEAT = L_TOK + 12
L_CMP = L_FEAT + 9
L_GATE = L_CMP + 5
L_OUT = L_GATE + 24
L_FFN2 = L_OUT + 4
LAYER_UNITS = L_FFN2 + 33
LAYER_TURNS = LAYER_UNITS // RING
assert LAYER_UNITS % RING == 0 and U_EXPERT % RING == 0 and U_LAYER % RING == 0

C_A, C_BX, C_CQ, C_KC, C_KS, C_G, C_DQ, C_DV, C_DG, C_GATES = 0, 768, 2304, 2816, 3072, 3584, 3608, 4120, 4632, 5144

PB_AQ, PB_AK, PB_AV, PB_CQ, PB_KS, PB_VS, PB_KW, PB_VW, PB_DQ, PB_DV, PB_G = (
    0, 512, 640, 768, 1280, 1408, 1536, 1664, 1792, 2304, 2816)
PB_W = PB_G + 24
NORMED = 1664
FB_K, FB_V, FB_CK, FB_CV, FB_U, FB_VV, FB_W = 512, 640, 768, 896, 1024, 1536, 2048

TILE_BY = "AVAVAVAVAVAA" + "VAVAVV" + "AAA"
TILES_A, TILES_V = TILE_BY.count("A"), TILE_BY.count("V")
B1_TILE_BY = "AVAVAAAA"
B1_A, B1_V = B1_TILE_BY.count("A"), B1_TILE_BY.count("V")

XB, XL = 10, 12
V2_LOADS = 21
OWN_V = 130

BRANCHES = (1, 3, 0, 2)
EARLY = 12


def gate_unit(i, j):
    if i == 0:
        return j
    if i == 1 and j < 2:
        return 4 + j
    return 6 * i + (j if j < 3 else 5)


def branch_unit(i):
    return 6 if i == 0 else 6 * i + 3



V1 = dict(g_mix=0, g_ffn=8, b_mod=16, c=64, c_ctx=72, b_s=80)
V1_N = 88
V2 = dict(ffn1=0, mix=8, ffn2=16, merge=24, conv=56, ret=68, aq=72, ak=73, cq=74, kc=75, ks=76, kw=77, pos=78)
V2_N = 110


def const_table():
    parts = []
    q = np.arange(P)[:, None]
    parts.append(("ident", np.eye(P)))
    bc = np.zeros((P, P))
    bc[0::32] = 1.0
    parts.append(("sum_rows", bc))
    parts.append(("stack", np.tile(np.eye(32), (4, 1))))
    pick = np.zeros((P, 2))
    pick[0::32, 0] = 1.0
    pick[16::32, 1] = 1.0
    parts.append(("pick", pick))
    k = np.arange(T)[None, :]
    parts.append(("causal0", np.where(k[:, :P] <= q, 0.0, NEG)))
    parts.append(("causal1", np.where(k <= q + P, 0.0, NEG)))
    parts.append(("window1", np.where((k <= q + P) & (k > q), 0.0, NEG)))
    end = np.arange(NCMP) * 16 + 31
    cm = [np.where(end[None, :] <= q + t * P, 0.0, NEG) for t in range(TT)]
    parts.append(("cmp", np.concatenate([c for c in cm for _ in range(4)], axis=1)))
    lg = np.log(1.0 - 2.0 ** (-5.0 - np.arange(4)))
    m, c = np.arange(P)[:, None], np.arange(P)[None, :]
    parts.append(("decay0", np.concatenate(
        [np.where(c >= m, np.exp(np.maximum(c - m, 0) * g), 0.0) * SCALE for g in lg], axis=1)))
    parts.append(("decay1", np.concatenate([np.exp((c + P - m) * g) * SCALE for g in lg], axis=1)))
    f32 = np.float32
    t = np.arange(T)
    inv1 = (f32(10000.0) ** (-np.arange(16, dtype=f32) / f32(16))).astype(f32)
    ang1 = np.concatenate([(t // 64).astype(f32)[:, None] * inv1, (t % 64).astype(f32)[:, None] * inv1], axis=1)
    inv2 = (f32(10000.0) ** (-np.arange(32, dtype=f32) / f32(32))).astype(f32)
    ang2 = t.astype(f32)[:, None] * inv2
    for name, ang in (("rope1", ang1), ("rope2", ang2)):
        for fn, tag in ((np.cos, "c"), (np.sin, "s")):
            parts.append((name + tag, fn(ang.astype(np.float64)).reshape(TT, P, 32).transpose(1, 0, 2).reshape(P, TT * 32)))
    parts.append(("iota", np.broadcast_to(np.arange(T)[None, :], (P, T))))
    at, n = {}, 0
    for name, a in parts:
        at[name] = (n, a.shape[1])
        n += a.shape[1]
    return np.ascontiguousarray(np.concatenate([a for _, a in parts], axis=1).astype(np.float32)), at


def build(nc, a, out, const, const_at):
    with ExitStack() as ctx:
        def sb(name, shape, dt=F32):
            return ctx.enter_context(nc.sbuf_tensor(name, shape, dt))

        def sem(name):
            return ctx.enter_context(nc.semaphore(name))

        ring = sb("ring", [P, RING, UNIT])
        cst = sb("cst", [P, const.shape[1]])
        X = sb("X", [P, TT, D])
        ZP = sb("ZP", [P, 2 * UNIT])
        ZT = sb("ZT", [P, KC, T])
        PB = sb("PB", [P, TT, PB_W])
        QT = sb("QT", [P, 4608])
        YT = sb("YT", [P, 4, 4, T])
        KCV = sb("KCV", [P, 2, T])
        BK = sb("BK", [P, 1032])
        GB = sb("GB", [P, 2, T])
        vcol = sb("vcol", [P, P])
        vrow = sb("vrow", [P, P])
        small = sb("small", [P, 512])
        ps = ctx.enter_context(nc.psum_tensor("banks", [P, 8, 512], F32))

        def C(name):
            n, w = const_at[name]
            return cst[:, n:n + w]

        ident = C("ident")
        Z = ZP[:, 0:UNIT].rearrange("p (t d) -> p t d", t=TT)
        MT = ZP[:, 0:UNIT].rearrange("p (c t) -> p c t", c=KC)
        PR = ZP[:, 0:UNIT].rearrange("p (b n) -> p b n", b=2)
        PT = ZP[:, UNIT:2 * UNIT].rearrange("p (b n) -> p b n", b=2)

        ss = small[:, 0:2]
        rstd = small[:, 2:4]
        hss = small[:, 4:60]
        hrs = small[:, 60:116]
        negmax = small[:, 116:124].rearrange("p (b h) -> p b h", b=2)
        den = small[:, 124:132].rearrange("p (b h) -> p b h", b=2)
        esink = small[:, 132:140].rearrange("p (b h) -> p b h", b=2)
        rden = small[:, 140:148].rearrange("p (b h) -> p b h", b=2)
        msink = small[:, 148:156].rearrange("p (b h) -> p b h", b=2)
        sinks = small[:, 156:164]
        nsinks = small[:, 164:172]
        cneg = small[:, 172:188]
        cden = small[:, 188:204]
        power = small[:, 204:205]
        eps = small[:, 205:206]
        modcol = small[:, 208:272]
        scaleA = small[:, 272:296].rearrange("p (i c) -> p i c", i=3)
        cs = small[:, 296:312]
        gmean = small[:, 312:320]
        kss = small[:, 320:321]
        krs = small[:, 321:322]
        idxcol = small[:, 322:338]
        gatecol = small[:, 338:354]
        lsum = small[:, 354:358]
        scaleB = small[:, 360:384].rearrange("p (i c) -> p i c", i=3)

        landed = [sem(f"unit_landed{i}") for i in range(RING)]
        unit_done = sem("unit_done")
        const_in = sem("const_in")
        x_in = sem("x_in")
        ctx_in = sem("ctx_in")
        vrow_in = sem("vrow_in")
        rows_in = sem("rows_in")
        ws_in = sem("ws_in")
        v2_in = sem("v2_in")
        out_sent = sem("out_sent")
        vsteps = sem("vector_steps")
        psteps = sem("pool_steps")
        cols_turned = sem("cols_turned")
        cols_copied = sem("cols_copied")
        c_silu = sem("c_silu")
        mod_lhs = sem("mod_lhs")
        part_copied = sem("part_copied")
        modcols_full = sem("modcols_full")
        modcols_out = sem("modcols_out")
        modrow_full = sem("modrow_full")
        modrow_out = sem("modrow_out")
        affine_set = sem("affine_set")
        x_updated = sem("x_updated")
        norm_squares = sem("norm_squares")
        norm_rstd = sem("norm_rstd")
        norm_scaled = sem("norm_scaled")
        norm_turned = sem("norm_turned")
        norm_out_a = sem("norm_out_scalar")
        norm_out_v = sem("norm_out_vector")
        tile_out_a = sem("tile_out_scalar")
        tile_out_v = sem("tile_out_vector")
        head_squares = sem("head_squares")
        head_sums = sem("head_sums")
        head_rstd = sem("head_rstd")
        heads_ready = sem("heads_ready")
        turn_full = sem("turn_full")
        turn_out_a = sem("turn_out_scalar")
        turn_out_v = sem("turn_out_vector")
        scores_full = sem("scores_full")
        row_max = sem("row_max")
        exp_done = sem("exp_done")
        p_turned = sem("p_turned")
        pt_out_a = sem("pt_out_scalar")
        pt_out_v = sem("pt_out_vector")
        att_full = sem("att_full")
        att_scaled = sem("att_scaled")
        y_full = sem("y_full")
        y_out = sem("y_out")

        aff_exp = sem("aff_exp")
        aff_max = sem("aff_max")
        aff_ready = sem("aff_ready")
        afft_full = sem("afft_full")
        blk_ready = sem("blk_ready")
        branch_full = sem("branch_full")
        cmp_cleared = sem("cmp_cleared")
        cmp_exp = sem("cmp_exp")
        cmp_full = sem("cmp_full")
        cmp_landed = sem("cmp_landed")
        cmp_out = sem("cmp_out")
        cmp_parts = sem("cmp_parts")
        cmp_pt = sem("cmp_pt")
        cmp_scores = sem("cmp_scores")
        cmp_shifted = sem("cmp_shifted")
        cmp_summed = sem("cmp_summed")
        cmp_turned = sem("cmp_turned")
        conv_ready = sem("conv_ready")
        ffn_full = sem("ffn_full")
        ffn_hidden = sem("ffn_hidden")
        ffn_silu = sem("ffn_silu")
        final_rstd = sem("final_rstd")
        final_squares = sem("final_squares")
        gate_even = sem("gate_even")
        gate_ready = sem("gate_ready")
        gate_stored = sem("gate_stored")
        gfinal_in = sem("gfinal_in")
        gm_full = sem("gm_full")
        gm_out = sem("gm_out")
        hid_ready = sem("hid_ready")
        ht_ready = sem("ht_ready")
        kc_rstd = sem("kc_rstd")
        kc_squares = sem("kc_squares")
        kcn_ready = sem("kcn_ready")
        kct_full = sem("kct_full")
        kct_out = sem("kct_out")
        kv_full = sem("kv_full")
        merged = sem("merged")
        moe_full = sem("moe_full")
        oh_ready = sem("oh_ready")
        pg_copied = sem("pg_copied")
        pu_copied = sem("pu_copied")
        ret_centred = sem("ret_centred")
        ret_copied = sem("ret_copied")
        ret_decayed = sem("ret_decayed")
        ret_full = sem("ret_full")
        ret_normed = sem("ret_normed")
        ret_rstd = sem("ret_rstd")
        ret_scores = sem("ret_scores")
        ret_squares = sem("ret_squares")
        ret_sums = sem("ret_sums")
        rope_ready = sem("rope_ready")
        scattered = sem("scattered")
        sel_ready = sem("sel_ready")
        sel_turned = sem("sel_turned")
        sg_ready = sem("sg_ready")
        slots_full = sem("slots_full")
        sums_full = sem("sums_full")
        top_ready = sem("top_ready")
        vb_ready = sem("vb_ready")
        vv_ready = sem("vv_ready")
        vv_rstd = sem("vv_rstd")
        vv_squares = sem("vv_squares")
        xe_full = sem("xe_full")
        xe_ready = sem("xe_ready")
        yd_out = sem("yd_out")
        ye_a = sem("ye_a")
        ye_v = sem("ye_v")
        zeros_set = sem("zeros_set")

        def slot(n):
            return ring[:, n % RING, :]

        def wait_unit(eng, n, turns=0):
            eng.wait_ge(landed[n % RING], turns * 16 + 16 * (n // RING + 1))

        def wait_done(eng, n, turns=0):
            eng.wait_ge(unit_done, turns * RING + (n + 1))

        def wait_tile(eng, m, by, na, nv):
            if by[m] == "A":
                eng.wait_ge(tile_out_a, na + by[:m + 1].count("A"))
            else:
                eng.wait_ge(tile_out_v, nv + by[:m + 1].count("V"))

        block = ctx.enter_context(nc.Block())
        XC = QT[:, 0:UNIT].rearrange("p (t d) -> p t d", t=TT)
        qT1 = QT[:, 0:1024].rearrange("p (c t) -> p c t", c=4)
        kT1 = QT[:, 1024:2048].rearrange("p (g t) -> p g t", g=2)
        wsT = QT[:, 2048:3072].rearrange("p (g i) -> p g i", g=8)
        wsR = QT[:, 3072:4096].rearrange("p (g i) -> p g i", g=8)
        YF = YT[:].rearrange("p b c t -> p (b c t)")
        CT = YF[:, 0:2048].rearrange("p (c t) -> p c t", c=KC)
        GT = YF[:, 2048:4096].rearrange("p (i d) -> p i d", i=2)
        PBf = PB[:].rearrange("p t n -> p (t n)")
        B1 = PBf[:, 0:TT * FB_W].rearrange("p (t n) -> p t n", t=TT)
        SQ1 = ZP[:, 2048:2048 + TT * 896].rearrange("p (t n) -> p t n", t=TT)
        modL = BK[:, 0:256].rearrange("p (k m) -> p k m", k=KC)
        vgain = BK[:, 256:768]
        qgain = BK[:, 768:832]
        kgain = BK[:, 832:896]
        GBf = GB[:].rearrange("p b t -> p (b t)")
        KCVf = KCV[:].rearrange("p g t -> p (g t)")
        PART = [GBf, KCVf]
        KN1 = ZP[:, 0:1024].rearrange("p (s g u d) -> p s g u d", s=4, g=2, u=2)
        RQ1 = ZP[:, 1024:2048].rearrange("p (t h d) -> p t h d", t=TT, h=8)
        RT1 = ZP[:, 2048:3328].rearrange("p (i t h d) -> p i t h d", i=2, t=TT, h=10)
        XE = BK[:, 0:256].rearrange("p (k s) -> p k s", k=KC)
        OH = BK[:, 256:320].rearrange("p (t s) -> p t s", t=TT)
        SG = BK[:, 320:448]
        SEL = BK[:, 512:768]
        SELG = BK[:, 768:1024]
        HT = GBf.rearrange("p (f s) -> p f s", f=16)
        PG = [PBf[:, 512 * i:512 * i + 512] for i in range(4)]
        YE = PBf[:, 2048:3072]
        AFF = PBf[:, 3072:3104].rearrange("p (t e) -> p t e", t=TT)
        AFFT = PBf[0:NE, 3104:3360]
        WORK = PBf[0:NE, 3360:3616]
        VALS = PBf[0:NE, 3616:3648]
        IDX = PBf[0:NE, 3648:3680].bitcast(U32)
        REPI = PBf[0:NE, 3680:3808]
        REPV = PBf[0:NE, 3808:3936]
        gfinal = PBf[:, 4096:5120]
        zeros = PBf[:, 5120:5632]
        SQ2 = ZP[:, 0:TT * NORMED].rearrange("p (t n) -> p t n", t=TT)
        KN = ZP[:, 0:1536].rearrange("p (t k g u d) -> p t k g u d", t=TT, k=3, g=2, u=2)
        RTa = ZP[:, 1536:2048].rearrange("p (t h d) -> p t h d", t=TT, h=8)
        RTb = GBf.rearrange("p (t h d) -> p t h d", t=TT, h=8)
        BX = ZP[:, 2048:3072].rearrange("p (c t) -> p c t", c=4)
        RQ = ZP[:, 3072:4096].rearrange("p (t h d) -> p t h d", t=TT, h=8)
        aqT = QT[:, 0:1024].rearrange("p (c t) -> p c t", c=4)
        cqT = QT[:, 1024:2048].rearrange("p (c t) -> p c t", c=4)
        kT = QT[:, 2048:3584].rearrange("p (k g t) -> p k g t", k=3, g=2)
        dT = QT[:, 3584:4608].rearrange("p (c t) -> p c t", c=4)
        ZC = BK[:, 0:1032].rearrange("p (c t) -> p c t", c=4)
        BLK = BK[:, 0:960].rearrange("p (l g n) -> p l g n", l=32, g=2)
        PC = YF[:, 2048:2560]
        PCv = PC.rearrange("p (h n) -> p h n", h=16)
        VB = YF[:, 2560:2816]
        PTC = GBf
        HC = vrow[:, 0:120].rearrange("p (s h n) -> p s h n", s=2, h=2)
        KCN = BK[0:30, 0:128].rearrange("p (u d) -> p u d", u=2)
        kcT = BK[:, 128:158]
        AT = ZP[:, 0:1536].rearrange("p (i n) -> p i n", i=3)
        EG = [QT[:, 3584 + T * c:3584 + T * c + T] for c in range(4)] + [KCV[:, c, :] for c in range(2)]
        EG += [BK[:, 512 + T * c:512 + T * c + T] for c in range(2)] + [QT[:, T * c:T * c + T] for c in range(4)]
        FS = ZP[:, 2048:3072].rearrange("p (i t) -> p i t", i=4)
        FH = ZP[:, 3072:4096].rearrange("p (i t) -> p i t", i=4)

        class Steps:

            def __init__(self, eng, semaphore):
                self.eng, self.sem, self.n, self.base = eng, semaphore, 0, 0

            def __call__(self, instruction):
                instruction.then_inc(self.sem, 1)
                self.n += 1

            def settle(self):
                self.eng.wait_ge(self.sem, self.base + self.n)

            def loop(self, var, times, per):
                self.outer = (self.n, times, per)
                self.base = self.base + var * per

            def end(self):
                n, times, per = self.outer
                assert self.n - n == per, f"{self.sem}: {self.n - n} steps a turn, not {per}"
                self.base, self.n = 0, n + times * per

        @block.sync
        def _(sp):
            def load(n, dst, src, turns=0):
                if n >= RING or not isinstance(turns, int):
                    sp.wait_ge(unit_done, turns * RING + (n - RING + 1))
                sp.dma_start(dst, src).then_inc(landed[n % RING], 16)

            def cols256(n, w, c0, turns=0):
                load(n, slot(n).rearrange("p (k n) -> p k n", k=KC),
                     w[:, c0:c0 + 256].rearrange("(k p) n -> p k n", p=P), turns)

            def rows256(n, w, r0, turns=0):
                load(n, slot(n).rearrange("p (k n) -> p k n", k=2),
                     w[r0:r0 + 256, :].rearrange("(k p) n -> p k n", p=P), turns)

            def layer_vectors(l):
                def vec(name, key, n, per, off=0):
                    flat = a[name]
                    while len(flat.shape) > 1:
                        names = " ".join("abcd"[:len(flat.shape)])
                        flat = flat.rearrange(f"{names} -> ({names})")
                    sp.dma_start(vrow[V2[key]:V2[key] + n, :],
                                  flat[l * per + off:l * per + off + n * P].rearrange("(k p) -> k p", p=P)).then_inc(v2_in, 16)

                vec("ffn1_norm_2", "ffn1", 8, D)
                vec("mix_norm_2", "mix", 8, D)
                vec("ffn2_norm_2", "ffn2", 8, D)
                vec("merge_gate_bias_2", "merge", 32, 4 * D)
                vec("conv_w_2", "conv", 12, 3 * 512)
                vec("ret_norm_gain_2", "ret", 4, 512)
                for key, name, off, per in (("aq", "swa_q_gain_2", 0, HD), ("ak", "swa_k_gain_2", 0, HD),
                                            ("cq", "nsa_q_gain_2", 0, HD), ("kc", "nsa_k_gain_2", 0, 3 * HD),
                                            ("ks", "nsa_k_gain_2", HD, 3 * HD), ("kw", "nsa_k_gain_2", 2 * HD, 3 * HD)):
                    g = a[name]
                    g = g.rearrange("a b -> (a b)") if len(g.shape) == 2 else g.rearrange("a b c -> (a b c)")
                    for u in range(2):
                        sp.dma_start(vrow[V2[key]:V2[key] + 1, HD * u:HD * u + HD],
                                      g[l * per + off:l * per + off + HD].unsqueeze(0)).then_inc(v2_in, 16)
                for u, name in enumerate(("cmp_pos_k_2", "cmp_pos_v_2")):
                    sp.dma_start(vrow[V2["pos"]:V2["pos"] + 32, HD * u:HD * u + HD],
                                  a[name].rearrange("l r d -> (l r) d")[l * 32:l * 32 + 32, :]).then_inc(v2_in, 16)
                sp.dma_start(sinks, a["swa_sinks_2"].rearrange("l h -> (l h)")[l * 8:l * 8 + 8].partition_broadcast(P)
                              ).then_inc(v2_in, 16)

            w_mod = a["w_mod"][0]
            for u in range(24):
                half, ch = u % 2, u // 2
                load(U_MOD + u, slot(u).rearrange("p (k n) -> p k n", k=4),
                     w_mod[512 * half:512 * half + 512, 512 * ch:512 * ch + 512].rearrange("(k p) n -> p k n", p=P))
            w_in = a["w_in"][0]
            for u in range(7):
                cols256(U_WIN + u, w_in, 256 * u)
            for u in range(4):
                rows256(U_WOUT + u, a["w_out"][0], 256 * u)
            load(U_ROUTER, slot(U_ROUTER)[:, 0:KC * NE].rearrange("p (k n) -> p k n", k=KC),
                 a["w_router"][0].rearrange("(k p) n -> p k n", p=P))

            sp.wait_ge(cols_copied, 1)
            layer_vectors(0)

            w1 = a["w1"].rearrange("l e d f -> (l e d) f")
            w3 = a["w3"].rearrange("l e d f -> (l e d) f")
            w2 = a["w2"].rearrange("l e f d -> (l e f) d")
            with sp.Fori(0, NE) as e:
                for u in range(16):
                    ch, w, half = u // 4, (w1, w3)[u // 2 % 2], u % 2
                    load(U_EXPERT + u, slot(u).rearrange("p (k n) -> p k n", k=4),
                         w[bass.ds(e * D + 512 * half, 512), 512 * ch:512 * ch + 512].rearrange("(k p) n -> p k n", p=P),
                         e * 2)
                for u in range(8):
                    load(U_EXPERT + 16 + u, slot(16 + u).rearrange("p (k n) -> p k n", k=2),
                         w2[bass.ds(e * EFF + 256 * u, 256), :].rearrange("(k p) n -> p k n", p=P), e * 2)

            gates = [a[f"ffn{i}_w_gate_2"].rearrange("l d f -> (l d) f") for i in (1, 2)]
            ups = [a[f"ffn{i}_w_up_2"].rearrange("l d f -> (l d) f") for i in (1, 2)]
            downs = [a[f"ffn{i}_w_down_2"].rearrange("l f d -> (l f) d") for i in (1, 2)]
            w_in2 = a["w_in_2"].rearrange("l d n -> (l d) n")
            w_br = a["w_branch_2"].rearrange("l b w d -> (l b w) d")
            w_out2 = a["w_out_2"].rearrange("l d n -> (l d) n")
            with sp.Fori(0, NL) as l:
                turns = l * LAYER_TURNS

                def cols(n, w, c0, c1=None):
                    c1 = c0 + 256 if c1 is None else c1
                    load(U_LAYER + n, slot(n)[:, 0:KC * (c1 - c0)].rearrange("p (k n) -> p k n", k=KC),
                         w[bass.ds(l * D, D), c0:c1].rearrange("(k p) n -> p k n", p=P), turns)

                def ffn(first, i):
                    def step(u, turn, done):
                        n = U_LAYER + first + 3 * u
                        for j, w in enumerate((gates[i], ups[i])):
                            load(n + j, slot(n + j).rearrange("p (k n) -> p k n", k=KC),
                                 w[bass.ds(l * D, D), bass.ds(done + 256 * u, 256)].rearrange("(k p) n -> p k n", p=P), turn)
                        load(n + 2, slot(n + 2).rearrange("p (k n) -> p k n", k=2),
                             downs[i][bass.ds(l * FF + done + 256 * u, 256), :].rearrange("(k p) n -> p k n", p=P), turn)

                    with sp.Fori(0, 2) as b:
                        for u in range(4):
                            step(u, turns + b, b * 1024)
                    for u in range(8, 11):
                        step(u, turns, 0)

                ffn(L_FFN1, 0)
                for i, c0 in enumerate([0, 256, 512, C_CQ, C_CQ + 256, C_KS, C_KS + 256, C_DQ, C_DQ + 256, C_DV, C_DV + 256]):
                    cols(L_TOK + i, w_in2, c0)
                cols(L_TOK + 11, w_in2, C_G, C_G + 24)
                for i, c0 in enumerate([C_BX + 256 * j for j in range(6)] + [C_KC, C_DG, C_DG + 256]):
                    cols(L_FEAT + i, w_in2, c0)
                for i in range(4):
                    n = U_LAYER + L_CMP + i
                    sp.wait_ge(unit_done, turns * RING + (n - RING + 1))
                    for half, name in enumerate(("cmp_wk1_2", "cmp_wv1_2")):
                        w = a[name].rearrange("l r h -> (l r) h")
                        sp.dma_start(slot(n)[64 * half:64 * half + 64, :].rearrange("p (k n) -> p k n", k=8),
                                     w[bass.ds(l * 2048 + 512 * i, 512), :].rearrange("(k p) n -> p k n", p=64)
                                     ).then_inc((cmp_landed, landed[n % RING])[half], 16)
                n = U_LAYER + L_CMP + 4
                sp.wait_ge(unit_done, turns * RING + (n - RING + 1))
                for half, name in enumerate(("cmp_wk2_2", "cmp_wv2_2")):
                    w = a[name].rearrange("l r h -> (l r) h")
                    sp.dma_start(slot(n)[:, 128 * half:128 * half + 128].rearrange("p (k n) -> p k n", k=2),
                                 w[bass.ds(l * 256, 256), :].rearrange("(k p) n -> p k n", p=P)
                                 ).then_inc((cmp_landed, landed[n % RING])[half], 16)
                units = {gate_unit(i, j): (True, b, j) for i, b in enumerate(BRANCHES) for j in range(4)}
                units |= {branch_unit(i) + j: (False, b, j) for i, b in enumerate(BRANCHES) for j in range(2)}
                for g in range(24):
                    of_gates, b, j = units[g]
                    if of_gates:
                        cols(L_GATE + g, w_in2, C_GATES + 1024 * b + 256 * j)
                    else:
                        load(U_LAYER + L_GATE + g, slot(L_GATE + g).rearrange("p (k n) -> p k n", k=2),
                             w_br[bass.ds(l * 2048 + 512 * b + 256 * j, 256), :].rearrange("(k p) n -> p k n", p=P), turns)
                for j in range(4):
                    load(U_LAYER + L_OUT + j, slot(L_OUT + j).rearrange("p (k n) -> p k n", k=2),
                         w_out2[bass.ds(l * D + 256 * j, 256), :].rearrange("(k p) n -> p k n", p=P), turns)
                sp.wait_ge(gate_ready, l * 32 + 1)
                layer_vectors(1)
                ffn(L_FFN2, 1)

            sp.wait_ge(x_updated, XB + XL * NL)
            for t in range(TT):
                sp.dma_start(out[0, P * t:P * t + P, :], X[:, t, :]).then_inc(out_sent, 16)
            sp.wait_ge(v2_in, 16 * V2_LOADS * (NL + 1))
            sp.wait_ge(out_sent, 16 * TT)

        @block.tensor
        def _(pe):
            mm, tr = nc.tensor.matmul, nc.tensor.transpose

            pe.wait_ge(const_in, 16)
            pe.wait_ge(vrow_in, 16 * 6)
            tr(ps[:, 0, 0:V1_N], vrow[0:V1_N, :], ident[0:V1_N, 0:V1_N]).then_inc(cols_turned, 1)

            pe.wait_ge(mod_lhs, 2)
            with pe.Fori(0, 2) as i:
                def mod_part(m):
                    bank = 4 + m % 2
                    if m >= 2:
                        pe.wait_ge(part_copied, i * 6 + (m - 1))
                    elif m < 2:
                        pe.wait_ge(part_copied, i * 6)
                    for k in range(KC):
                        if k % 4 == 0:
                            wait_unit(pe, U_MOD + 2 * m + k // 4, i)
                        j = k % 4
                        last = mm(ps[32 * j:32 * j + 32, bank, :], modL[:, k, :],
                                  slot(2 * m + k // 4)[:, 512 * j:512 * j + 512], start=(k < 4), stop=(k >= 4))
                        if j == 3:
                            last.then_inc(unit_done, 1)

                def mod_sum(m):
                    pe.wait_ge(part_copied, i * 6 + (m + 1))
                    if m < 4:
                        if m == 0:
                            pe.wait_ge(modcols_out, i)
                        for n in range(4):
                            c = 2 * (8 * (m // 2) + 4 * (m % 2) + n)
                            last = mm(ps[:, 6, c:c + 2], PART[m % 2][:, P * n:P * n + P], C("pick"), start=True, stop=True)
                        last.then_inc(modcols_full, 1)
                    else:
                        pe.wait_ge(modrow_out, i * 2 + (m - 4))
                        mm(ps[:, 7, :], C("sum_rows"), PART[m % 2], start=True, stop=True).then_inc(modrow_full, 1)

                for m in range(6):
                    mod_part(m)
                    if m:
                        mod_sum(m - 1)
                mod_sum(5)

            def norm(v):
                if not isinstance(v, int) or v:
                    pe.wait_ge(norm_out_a, v * 4)
                    pe.wait_ge(norm_out_v, v * 4)
                pe.wait_ge(norm_scaled, v * 2 + 2)
                for b in range(4):
                    for c in range(2):
                        for t in range(TT):
                            last = tr(ps[:, b, 256 * c + P * t:256 * c + P * t + P],
                                      Z[:, t, P * (2 * b + c):P * (2 * b + c) + P], ident)
                    last.then_inc(norm_turned, 1)

            def normed(v):
                pe.wait_ge(norm_out_a, v * 4 + 4)
                pe.wait_ge(norm_out_v, v * 4 + 4)

            def tok_tile(src, n, bank, width):
                for t in range(TT):
                    for k in range(KC):
                        last = mm(ps[:, bank, width * t:width * t + width], src[:, k, P * t:P * t + P],
                                  slot(n)[:, width * k:width * k + width], start=(k == 0), stop=(k == KC - 1))
                return last

            norm(0)
            norm(1)
            normed(1)
            for m, u in enumerate((0, 1, 2, 2, 3, 4, 5, 6)):
                if m >= 4:
                    wait_tile(pe, m - 4, B1_TILE_BY, 0, 0)
                wait_unit(pe, U_WIN + u)
                last = tok_tile(CT if m == 3 else ZT, U_WIN + u, 4 + m % 4, 256)
                last.then_inc(kv_full if m == 2 else unit_done, 1)

            pe.wait_ge(ws_in, 16)
            for n in range(2):
                for g in range(4):
                    last = tr(ps[:, n, P * g:P * g + P], wsR[:, 4 * n + g, :], ident)
                last.then_inc(turn_full, 1)
            pe.wait_ge(heads_ready, 1)
            for n in range(2):
                for c in range(2):
                    for t in range(TT):
                        last = tr(ps[:, 2 + n, 256 * c + P * t:256 * c + P * t + P],
                                  RQ1[:, t, 2 * (2 * n + c):2 * (2 * n + c) + 2, :].rearrange("p h d -> p (h d)"), ident)
                last.then_inc(turn_full, 1)
            pe.wait_ge(turn_out_a, 1)
            pe.wait_ge(turn_out_v, 1)
            for g in range(2):
                for s in range(4):
                    last = tr(ps[:, g, P * s:P * s + P], KN1[:, s, g].rearrange("p u d -> p (u d)"), ident)
                last.then_inc(turn_full, 1)

            def attention(units, base, scores, between=None):
                def turn(i, unit):
                    heads, keys = unit[1], unit[2]
                    pe.wait_ge(exp_done, base + (i + 1))
                    pe.wait_ge(pt_out_a, base + i)
                    pe.wait_ge(pt_out_v, base + i)
                    n = heads * keys
                    for b in range(n):
                        last = tr(ps[:, 4 + b // (n // 2), P * (b % (n // 2)):P * (b % (n // 2)) + P],
                                  PR[:, i % 2, P * b:P * b + P], ident)
                        if b % (n // 2) == n // 2 - 1:
                            last.then_inc(p_turned, 1)

                def weigh(i, unit):
                    heads, keys, value = unit[1], unit[2], unit[3]
                    pe.wait_ge(pt_out_a, base + (i + 1))
                    pe.wait_ge(pt_out_v, base + (i + 1))
                    pe.wait_ge(att_scaled, base + (i - 1)) if i else pe.wait_ge(att_scaled, base)
                    for h in range(heads):
                        for k in range(keys):
                            b = h * keys + k
                            last = mm(ps[:, 6 + i % 2, HD * h:HD * h + HD], PT[:, i % 2, P * b:P * b + P], value(k),
                                      start=(k == 0), stop=(k == keys - 1))
                    last.then_inc(att_full, 1)

                def score(i, unit):
                    pe.wait_ge(exp_done, base + (i - 1)) if i else pe.wait_ge(exp_done, base)
                    scores(i, unit)

                score(0, units[0])
                for i, unit in enumerate(units):
                    if i + 1 < len(units):
                        score(i + 1, units[i + 1])
                    turn(i, unit)
                    if between:
                        between(i)
                    weigh(i, unit)

            def scores1(i, unit):
                t, hp = unit[0], unit[4]
                g = hp // 2
                for h in range(2):
                    off = 64 * h
                    last = mm(ps[:, 2 * (i % 2) + h, :], qT1[off:off + 64, hp, P * t:P * t + P],
                              kT1[off:off + 64, g, :], start=True, stop=True)
                last.then_inc(scores_full, 1)

            def value1(g):
                return lambda k: (B1[:, k, FB_V + HD * g:FB_V + HD * g + HD] if k < 2
                                  else B1[:, k - 2, FB_CV + HD * g:FB_CV + HD * g + HD])

            pe.wait_ge(turn_out_a, 3)
            pe.wait_ge(turn_out_v, 3)
            attention([(t, 2, 4, value1(hp // 2), hp) for t in range(TT) for hp in range(4)], 0, scores1)

            pe.wait_ge(vv_ready, 2)
            pe.wait_ge(exp_done, 8)
            for t in range(TT):
                for g in range(8):
                    last = mm(ps[:, t, HD * g:HD * g + HD], wsT[:, g, :], B1[:, t, FB_VV + HD * g:FB_VV + HD * g + HD],
                              start=True, stop=True)
                last.then_inc(gm_full, 1)

            def turn_y(tiles, src, done, base):
                for n, j in enumerate(tiles):
                    if n >= 2:
                        pe.wait_ge(done, base + (n - 1))
                    for c in range(2):
                        for t in range(TT):
                            last = tr(ps[:, 2 + n % 2, 256 * c + P * t:256 * c + P * t + P],
                                      src[:, t, j + P * c:j + P * c + P], ident)
                    last.then_inc(y_full, 1)

            pe.wait_ge(att_scaled, 8)
            pe.wait_ge(gm_out, 2)
            turn_y((0, 256, FB_U, FB_U + 256), B1, y_out, 0)

            def project_out(n, turns, src):
                for k in range(KC):
                    if k % 2 == 0:
                        wait_unit(pe, n + k // 2, turns)
                    for half in range(2):
                        for t in range(TT):
                            last = mm(ps[:, 4 + 2 * t + half, :], src[:, k, P * t:P * t + P],
                                      slot(n + k // 2)[:, D * (k % 2) + 512 * half:D * (k % 2) + 512 * half + 512],
                                      start=(k == 0), stop=(k == KC - 1))
                    if k % 2:
                        last.then_inc(unit_done, 1)

            pe.wait_ge(y_out, 4)
            project_out(U_WOUT, 0, ZT)

            norm(2)
            normed(2)
            wait_unit(pe, U_ROUTER)
            tok_tile(ZT, U_ROUTER, 4, NE).then_inc(unit_done, 1)
            pe.wait_ge(aff_ready, 1)
            for t in range(TT):
                last = tr(ps[0:NE, 5, P * t:P * t + P], AFF[:, t, :], ident)
            last.then_inc(afft_full, 1)
            pe.wait_ge(top_ready, 2)
            tr(ps[:, 6, 0:NE], REPI, ident[0:NE, 0:NE])
            tr(ps[:, 6, NE:2 * NE], REPV, ident[0:NE, 0:NE]).then_inc(slots_full, 1)

            pe.wait_ge(zeros_set, 1)
            for b in range(4):
                mm(ps[:, b, :], ident, zeros, start=True, stop=False, skip_group_check=True)

            with pe.Fori(0, NE) as e:
                pe.wait_ge(sel_ready, e * 2 + 2)
                for t in range(TT):
                    last = tr(ps[:, 4, P * t:P * t + P], SEL[:, P * t:P * t + P], ident)
                last.then_inc(sel_turned, 1)
                pe.wait_ge(oh_ready, e + 1)
                for k in range(KC):
                    for t in range(TT):
                        last = mm(ps[:, 5, 32 * k:32 * k + 32], Z[:, t, P * k:P * k + P], OH[:, t, :],
                                  start=(t == 0), stop=(t == TT - 1))
                last.then_inc(xe_full, 1)
                pe.wait_ge(xe_ready, e + 1)

                def parts(ch):
                    for w in range(2):
                        if ch:
                            pe.wait_ge((pg_copied, pu_copied)[w], e * 4 + ch)
                        for k in range(KC):
                            n = 4 * ch + 2 * w + k // 4
                            if k % 4 == 0:
                                wait_unit(pe, U_EXPERT + n, e * 2)
                            j = k % 4
                            last = mm(ps[32 * j:32 * j + 32, 4 + w, :], XE[:, k, :], slot(n)[:, 512 * j:512 * j + 512],
                                      start=(k < 4), stop=(k >= 4))
                            if j == 3:
                                last.then_inc(unit_done, 1)

                def sums(ch):
                    pe.wait_ge(pg_copied, e * 4 + (ch + 1))
                    pe.wait_ge(pu_copied, e * 4 + (ch + 1))
                    if ch >= 2:
                        pe.wait_ge(ht_ready, e * 4 + (ch - 1))
                    for w in range(2):
                        for f in range(4):
                            c = P * w + 32 * f
                            last = mm(ps[:, 6 + ch % 2, c:c + 32], PG[2 * w + ch % 2][:, P * f:P * f + P], C("stack"),
                                      start=True, stop=True)
                    last.then_inc(sums_full, 1)

                for ch in range(4):
                    parts(ch)
                    if ch:
                        sums(ch - 1)
                sums(3)
                pe.wait_ge(pu_copied, e * 4 + 4)
                for q in range(4):
                    pe.wait_ge(ht_ready, e * 4 + (q + 1))
                    n = 16 + 2 * q
                    wait_unit(pe, U_EXPERT + n, e * 2)
                    wait_unit(pe, U_EXPERT + n + 1, e * 2)
                    for half in range(2):
                        for j in range(4):
                            f = 4 * q + j
                            w = slot(n + j // 2)
                            last = mm(ps[32 * j:32 * j + 32, 4 + half, :], HT[:, f, :],
                                      w[:, D * (j % 2) + 512 * half:D * (j % 2) + 512 * half + 512],
                                      start=(q == 0), stop=(q == 3))
                            if half and j >= 2:
                                last.then_inc(unit_done, 1)
                pe.wait_ge(ye_a, e + 1)
                pe.wait_ge(ye_v, e + 1)
                for t in range(TT):
                    for half in range(2):
                        last = mm(ps[:, 2 * t + half, :], SELG[:, P * t:P * t + P], YE[:, 512 * half:512 * half + 512],
                                  start=False, stop=False, skip_group_check=True)
                last.then_inc(scattered, 1)
            for b in range(4):
                last = mm(ps[:, b, :], ident, zeros, start=False, stop=True, skip_group_check=True)
            last.then_inc(moe_full, 1)

            with pe.Fori(0, NL) as l:
                turns = l * LAYER_TURNS

                def ffn(f, first):
                    def gate_up(q, turn):
                        n = U_LAYER + first + 3 * (q // 2)
                        for w in range(2):
                            if q % 2 == 0:
                                wait_unit(pe, n + w, turn)
                            for k in range(KC):
                                last = mm(ps[:, 4 + q % 4, 256 * w:256 * w + 256],
                                          slot(n + w)[:, 256 * k + P * (q % 2):256 * k + P * (q % 2) + P], ZT[:, k, :],
                                          start=(k == 0), stop=(k == KC - 1))
                        last.then_inc(ffn_full, 1)

                    def down(q, done, turn):
                        n = U_LAYER + first + 3 * (q // 2)
                        pe.wait_ge(ffn_hidden, done + (q + 1))
                        if q % 2 == 0:
                            wait_unit(pe, n + 2, turn)
                        for half in range(2):
                            for t in range(TT):
                                last = mm(ps[:, 2 * t + half, :], FH[:, q % 4, P * t:P * t + P],
                                          slot(n + 2)[:, D * (q % 2) + 512 * half:D * (q % 2) + 512 * half + 512],
                                          start=(q == 0), stop=(q == FCH - 1), skip_group_check=True)
                                if half == 1 and (q % 2 == 0 or t == 1):
                                    last.then_inc(unit_done, 1)

                    done = f * FCH
                    gate_up(0, turns)
                    gate_up(1, turns)
                    down(0, done, turns)
                    with pe.Fori(0, 2) as b:
                        for q in range(1, 9):
                            gate_up(q + 1, turns + b)
                            down(q, done + b * 8, turns + b)
                    for q in range(17, FCH):
                        if q + 1 < FCH:
                            gate_up(q + 1, turns)
                        down(q, done, turns)

                pe.wait_ge(x_updated, l * XL + XB)
                pe.wait_ge(v2_in, l * 16 * V2_LOADS + 16 * V2_LOADS)
                tr(ps[:, 7, 0:V2_N], vrow[0:V2_N, :], ident[0:V2_N, 0:V2_N]).then_inc(cols_turned, 1)

                norm(l * 3 + 3)
                normed(l * 3 + 3)
                ffn(l * 2, L_FFN1)
                norm(l * 3 + 4)
                normed(l * 3 + 4)

                na, nv = l * TILES_A + B1_A, l * TILES_V + B1_V
                for m in range(21):
                    n = U_LAYER + L_TOK + m
                    if m >= 4:
                        wait_tile(pe, m - 4, TILE_BY, na, nv)
                    wait_unit(pe, n, turns)
                    if m < 11:
                        last = tok_tile(ZT, n, 4 + m % 4, 256)
                    elif m == 11:
                        last = tok_tile(ZT, n, 4 + m % 4, 24)
                    else:
                        for c in range(2):
                            for k in range(KC):
                                w = slot(n)[:, 256 * k:256 * k + 256]
                                if m != 18:
                                    last = mm(ps[:, 4 + m % 4, 256 * c:256 * c + 256], w[:, P * c:P * c + P], ZT[:, k, :],
                                              start=(k == 0), stop=(k == KC - 1))
                                    continue
                                for s in range(2):
                                    last = mm(ps[64 * s:64 * s + 64, 4 + m % 4, 256 * c:256 * c + 256],
                                              w[:, P * s + HD * c:P * s + HD * c + HD], ZT[:, k, :],
                                              start=(k == 0), stop=(k == KC - 1))
                    last.then_inc(unit_done, 1)

                def heads2(view, t, c):
                    return view[:, t, P * c:P * c + P]

                rq = RQ.rearrange("p t h d -> p t (h d)")
                src = [heads2(PB, t, PB_AQ // P + c) for c in range(4) for t in range(TT)]
                src += [heads2(PB, t, PB_CQ // P + c) for c in range(4) for t in range(TT)]
                src += [KN[:, t, k, g].rearrange("p u d -> p (u d)") for k in range(3) for g in range(2) for t in range(TT)]
                src += [heads2(rq, t, c) for c in range(4) for t in range(TT)]
                ta, tv = l * 5 + 3, l * 4 + 3
                pe.wait_ge(heads_ready, l + 2)
                for n in range(9):
                    if n == 7:
                        pe.wait_ge(rope_ready, l + 1)
                    if n >= 4:
                        if n % 2 == 0:
                            pe.wait_ge(turn_out_a, ta + (n - 4) // 2 + 1)
                        else:
                            pe.wait_ge(turn_out_v, tv + (n - 5) // 2 + 1)
                    if n == 8:
                        pe.wait_ge(blk_ready, l + 1)
                        wait_tile(pe, 20, TILE_BY, na, nv)
                        pe.wait_ge(cmp_landed, l * 80 + 80)
                        for i in range(4):
                            wait_unit(pe, U_LAYER + L_CMP + i, turns)
                    for j in range(4):
                        last = tr(ps[:, n % 4, P * j:P * j + P], src[4 * n + j], ident)
                    last.then_inc(turn_full, 1)

                for i in range(4):
                    n = U_LAYER + L_CMP + i
                    for j in range(8):
                        for s in range(2):
                            q, b0 = 32 * (j % 4), 2 * NCMP * (8 * i + j)
                            last = mm(ps[q:q + 32, 4 + s, 0:256], BK[64 * s:64 * s + 64, b0:b0 + 32],
                                      slot(n)[64 * s:64 * s + 64, 256 * j:256 * j + 256],
                                      start=(i == 0 and j < 4), stop=(i == 3 and j >= 4))
                    last.then_inc(unit_done, 1)
                pe.wait_ge(cmp_parts, l + 1)
                for s in range(2):
                    for hh in range(2):
                        last = mm(ps[:, 4 + 2 * s + hh, 0:30], GB[:, s, P * hh:P * hh + P], C("stack")[:, 0:30],
                                  start=True, stop=True)
                last.then_inc(cmp_summed, 1)
                n = U_LAYER + L_CMP + 4
                wait_unit(pe, n, turns)
                pe.wait_ge(hid_ready, l * 4 + 4)
                for hh in range(2):
                    last = mm(ps[0:30, 4, 0:HD], HC[:, 0, hh, :], slot(n)[:, HD * hh:HD * hh + HD],
                              start=(hh == 0), stop=(hh == 1))
                for g in range(2):
                    for hh in range(2):
                        last = mm(ps[0:NCMP, 5, HD * g:HD * g + HD], HC[:, 1, hh, NCMP * g:NCMP * g + NCMP],
                                  slot(n)[:, P + HD * hh:P + HD * hh + HD], start=(hh == 0), stop=(hh == 1))
                last.then_inc(unit_done, 1)
                pe.wait_ge(kcn_ready, l + 1)
                mm(ps[:, 6, 0:30], KCN.rearrange("p u d -> p (u d)"), ident[0:30, 0:30], start=True, stop=True
                   ).then_inc(kct_full, 1)

                pe.wait_ge(turn_out_a, ta + 5)
                pe.wait_ge(turn_out_v, tv + 4)
                for i, (tk, tq) in enumerate(((0, 0), (0, 1), (1, 1))):
                    for h in range(4):
                        off = 64 * (h % 2)
                        c = 256 * (i % 2) + P * (h // 2)
                        last = mm(ps[:, 2 * (i // 2) + h % 2, c:c + P], dT[off:off + 64, 2 + h // 2, P * tk:P * tk + P],
                                  dT[off:off + 64, h // 2, P * tq:P * tq + P], start=True, stop=True)
                    if i:
                        last.then_inc(ret_scores, 1)
                pe.wait_ge(ret_decayed, l * 6 + 6)
                pe.wait_ge(vb_ready, l + 1)
                pe.wait_ge(kct_out, l + 1)
                for tq in range(TT):
                    for h in range(4):
                        for tk in range(tq + 1):
                            last = mm(ps[:, 4 + tq, P * h:P * h + P], AT[:, tq + tk, P * h:P * h + P],
                                      PB[:, tk, PB_DV + P * h:PB_DV + P * h + P], start=(tk == 0), stop=(tk == tq))
                    last.then_inc(ret_full, 1)
                pe.wait_ge(ret_copied, l * 2 + 2)

                ua = l * 12 + 8

                def scores2(qT, kind):
                    def scores(i, unit):
                        t, _, keys, _, g = unit
                        for h in range(4):
                            hq = 4 * g + h
                            off = 64 * (hq % 2)
                            c = 256 * (h // 2)
                            last = mm(ps[:, 2 * (i % 2) + h % 2, c:c + P * keys],
                                      qT[off:off + 64, hq // 2, P * t:P * t + P],
                                      kT[off:off + 64, kind, g, 0:P * keys], start=True, stop=True)
                        last.then_inc(scores_full, 1)
                    return scores

                def value2(col, g):
                    return lambda k: PB[:, k, col + HD * g:col + HD * g + HD]

                def gate_sums(q, out):
                    i, c = q // KC, q % KC
                    n = U_LAYER + L_GATE + gate_unit(i, c // 2)
                    if c % 2 == 0:
                        wait_unit(pe, n, turns)
                    for k in range(KC):
                        last = mm(out, slot(n)[:, 256 * k + P * (c % 2):256 * k + P * (c % 2) + P], ZT[:, k, :],
                                  start=(k == 0), stop=(k == KC - 1))
                    last.then_inc(unit_done if c % 2 else gate_even, 1)

                def early_gate(q):
                    pe.wait_ge(gate_stored, l * EARLY + (q - 1)) if q >= 2 else pe.wait_ge(gate_stored, l * EARLY)
                    pe.wait_ge(att_scaled, l * 12 + (8 + q - 1)) if q >= 2 else pe.wait_ge(att_scaled, l * 12 + 8)
                    gate_sums(q, ps[:, 6 + q % 2, 256:512])

                def causal(qT, kind, col, base, early):
                    attention([(t, 4, t + 1, value2(col, g), g) for t in range(TT) for g in range(2)], base,
                              scores2(qT, kind), lambda i: early_gate(early + i))

                ya = l * 4 + 4
                causal(aqT, 0, PB_AV, ua, 0)
                pe.wait_ge(att_scaled, ua + 4)
                turn_y((PB_AQ, PB_AQ + 256), PB, y_out, ya)

                for t in range(TT):
                    for h in range(8):
                        off = 64 * (h % 2)
                        c = 32 * (4 * t + h // 2)
                        last = mm(ps[:, h % 2, c:c + NCMP], cqT[off:off + 64, h // 2, P * t:P * t + P],
                                  kcT[off:off + 64, NCMP * (h // 4):NCMP * (h // 4) + NCMP], start=True, stop=True)
                last.then_inc(cmp_scores, 1)
                pe.wait_ge(cmp_exp, l + 1)
                for i in range(4):
                    last = tr(ps[:, 4, P * i:P * i + P], PC[:, P * i:P * i + P], ident)
                last.then_inc(cmp_turned, 1)
                pe.wait_ge(cmp_pt, l + 1)
                pe.wait_ge(gate_stored, l * EARLY + 4)
                for t in range(TT):
                    for r in range(2):
                        i = 2 * r + t
                        last = mm(ps[:, 6 + t, 256 * r:256 * r + 256], PTC[:, P * i:P * i + P], VB, start=True, stop=True)
                last.then_inc(cmp_full, 1)
                pe.wait_ge(cmp_out, l * 2 + 2)

                pe.wait_ge(y_out, ya + 2)
                causal(cqT, 1, PB_VS, ua + 4, 4)
                causal(cqT, 2, PB_VW, ua + 8, 8)
                pe.wait_ge(att_scaled, ua + 12)
                pe.wait_ge(y_out, ya + 2)
                turn_y((PB_CQ, PB_CQ + 256), PB, y_out, ya + 2)
                pe.wait_ge(y_out, ya + 4)
                pe.wait_ge(ret_normed, l + 1)
                turn_y((PB_DQ, PB_DQ + 256), PB, yd_out, l * 2)

                pe.wait_ge(yd_out, l * 2 + 2)
                pe.wait_ge(conv_ready, l * 4 + 4)
                pe.wait_ge(gate_stored, l * EARLY + EARLY)
                for i, b in enumerate(BRANCHES):
                    for c in range(KC):
                        q = 8 * i + c
                        br = U_LAYER + L_GATE + branch_unit(i)
                        if q >= 4:
                            pe.wait_ge(merged, l * 32 + (q - 3))
                        if c == 0:
                            wait_unit(pe, br, turns)
                            wait_unit(pe, br + 1, turns)
                        for k in range(4):
                            last = mm(ps[:, 4 + q % 4, 256:512],
                                      slot(br + k // 2)[:, D * (k % 2) + P * c:D * (k % 2) + P * c + P],
                                      YT[:, b, k, :], start=(k == 0), stop=(k == 3))
                            if c == KC - 1 and k % 2:
                                last.then_inc(unit_done, 1)
                        if q < EARLY and c < KC - 1:
                            last.then_inc(branch_full, 1)
                        if q >= EARLY:
                            gate_sums(q, ps[:, 4 + q % 4, 0:256])
                pe.wait_ge(merged, l * 32 + 32)
                project_out(U_LAYER + L_OUT, turns, MT)

                norm(l * 3 + 5)
                normed(l * 3 + 5)
                ffn(l * 2 + 1, L_FFN2)

        @block.scalar
        def _(act):
            fn = nc.scalar.activation

            for name, n in (("g_mix", 8), ("g_ffn", 8), ("b_mod", 48), ("c", 8), ("c_ctx", 8), ("b_s", 8)):
                src = a[name]
                src = src.rearrange("(k p) -> k p", p=P) if name == "c_ctx" else (
                    src[0] if name == "b_s" else src[0].rearrange("(k p) -> k p", p=P))
                act.dma_start(vrow[V1[name]:V1[name] + n, :], src).then_inc(vrow_in, 16)
            act.dma_start(cst[:], const).then_inc(const_in, 16)
            act.dma_start(X[:], a["x"][0].rearrange("(t p) d -> p t d", p=P)).then_inc(x_in, 16)
            act.dma_start(XC, a["ctx"][0].rearrange("(t p) d -> p t d", p=P)).then_inc(ctx_in, 16)
            for i in range(2):
                c0 = (3 * i + 2) * D
                act.dma_start(GT[:, i, :], a["b_mod"][0, c0:c0 + D].partition_broadcast(P)).then_inc(rows_in, 16)
            act.dma_start(vgain, a["v_gain"][0].partition_broadcast(P)).then_inc(rows_in, 16)
            act.dma_start(qgain, a["q_gain"][0].partition_broadcast(P)).then_inc(rows_in, 16)
            act.dma_start(kgain, a["k_gain"][0].partition_broadcast(P)).then_inc(rows_in, 16)
            act.dma_start(wsR, a["w_s"][0].rearrange("g i j -> i g j")).then_inc(ws_in, 16)

            def squares(v, src):
                if not isinstance(v, int) or v:
                    act.wait_ge(norm_turned, v * 4)
                for t in range(TT):
                    fn(Z[:, t, :], src[:, t, :], ACT.Square, scale=D ** -0.5,
                       accum_out=ss[:, t:t + 1]).then_inc(norm_squares, 1)

            def norm_out(v, dst, scale, bias=None):
                for b in (0, 2):
                    act.wait_ge(norm_turned, v * 4 + (b + 1))
                    for c in (2 * b, 2 * b + 1):
                        fn(dst[:, c, :], ps[:, b, 256 * (c % 2):256 * (c % 2) + 256], ACT.Identity, scale=scale(c),
                           bias=bias(c) if bias else 0.0).then_inc(norm_out_a, 1)

            act.wait_ge(x_in, 16)
            squares(0, X)
            act.wait_ge(cols_copied, 1)
            fn(cs, vcol[:, V1["c"]:V1["c"] + 16], ACT.Silu).then_inc(c_silu, 1)
            with act.Fori(0, 2) as i:
                for m in range(6):
                    wait_done(act, U_MOD + 2 * m + 1, i)
                    fn(PART[m % 2], ps[:, 4 + m % 2, :], ACT.Copy).then_inc(part_copied, 1)

            def col(table, i):
                return lambda c: table[:, i, c:c + 1]

            act.wait_ge(affine_set, 5)
            norm_out(0, ZT, col(scaleA, 0), col(scaleB, 0))
            act.wait_ge(ctx_in, 16)
            squares(1, XC)
            norm_out(1, CT, col(scaleA, 1), col(scaleB, 1))

            def tile1(m, func):
                if m == 2:
                    act.wait_ge(kv_full, 1)
                else:
                    wait_done(act, U_WIN + (0, 1, 2, 2, 3, 4, 5, 6)[m])
                fn(B1[:, :, 256 * m:256 * m + 256], ps[:, 4 + m % 4, :].rearrange("p (t n) -> p t n", t=TT), func
                   ).then_inc(tile_out_a, 1)

            tile1(0, ACT.Copy)
            tile1(2, ACT.Copy)
            act.wait_ge(tile_out_a, 2)
            act.wait_ge(tile_out_v, 2)
            fn(SQ1, B1[:, :, 0:896], ACT.Square, scale=HD ** -0.5).then_inc(head_squares, 1)
            for m in range(4, 8):
                tile1(m, ACT.Gelu)
            act.wait_ge(tile_out_a, 6)
            act.wait_ge(head_sums, 1)
            for t in range(TT):
                fn(PART[t], B1[:, t, FB_VV:FB_VV + 512], ACT.Square, scale=512 ** -0.5,
                   accum_out=lsum[:, t:t + 1]).then_inc(vv_squares, 1)

            def turn_copy(dst, n_full, bank, **kw):
                act.wait_ge(turn_full, n_full)
                if kw:
                    fn(dst, ps[:, bank, :], ACT.Identity, **kw).then_inc(turn_out_a, 1)
                else:
                    fn(dst, ps[:, bank, :], ACT.Copy).then_inc(turn_out_a, 1)

            turn_copy(QT[:, 2048:2560], 1, 0)
            turn_copy(QT[:, 0:512], 3, 2)
            turn_copy(QT[:, 1024:1536], 5, 0)

            def attention(units, base, first, exps):
                def pt_copy(i):
                    n = units[i][1] * units[i][2] // 2 * P
                    act.wait_ge(p_turned, base * 2 + (2 * i + 1))
                    fn(PT[:, i % 2, 0:n], ps[:, 4, 0:n], ACT.Copy).then_inc(pt_out_a, 1)

                def exp(i):
                    act.wait_ge(row_max, base + (i + 1))
                    if i >= 2 or not first:
                        act.wait_ge(att_scaled, base + (i - 1))
                        act.wait_ge(p_turned, base * 2 + 2 * (i - 1))
                    exps(i, units[i])

                exp(0)
                for i in range(len(units)):
                    if i + 1 < len(units):
                        exp(i + 1)
                    pt_copy(i)

            def exps1(i, unit):
                b = i % 2
                for h in range(2):
                    last = fn(PR[:, b, 512 * h:512 * h + 512], ps[:, 2 * b + h, :], ACT.Exp, scale=SCALE,
                              bias=negmax[:, b, h:h + 1], accum_out=den[:, b, h:h + 1])
                last.then_inc(exp_done, 1)

            attention([(t, 2, 4) for t in range(TT) for hp in range(4)], 0, True, exps1)

            def y_copy(dst, n, full):
                act.wait_ge(y_full, full)
                fn(dst, ps[:, 2 + n % 2, :].rearrange("p (c t) -> p c t", c=2), ACT.Copy).then_inc(y_out, 1)

            for n in range(4):
                y_copy(ZT[:, 2 * n:2 * n + 2, :], n, n + 1)

            act.wait_ge(x_updated, 4)
            act.dma_start(gfinal, a["g_final"].partition_broadcast(P)).then_inc(gfinal_in, 16)
            squares(2, X)
            norm_out(2, ZT, col(scaleA, 2), col(scaleB, 2))

            act.wait_ge(aff_max, 2)
            for t in range(TT):
                fn(AFF[:, t, :], ps[:, 4, NE * t:NE * t + NE], ACT.Exp, bias=hrs[:, t:t + 1],
                   accum_out=lsum[:, 2 + t:3 + t]).then_inc(aff_exp, 1)

            with act.Fori(0, NE) as e:
                def part_copy(ch):
                    wait_done(act, U_EXPERT + 4 * ch + 1, e * 2)
                    fn(PG[ch % 2], ps[:, 4, :], ACT.Copy).then_inc(pg_copied, 1)

                def silu(ch):
                    act.wait_ge(sums_full, e * 4 + (ch + 1))
                    act.wait_ge(ht_ready, e * 4 + ch)
                    fn(SG, ps[:, 6 + ch % 2, 0:P], ACT.Silu).then_inc(sg_ready, 1)

                for ch in range(4):
                    part_copy(ch)
                    if ch:
                        silu(ch - 1)
                silu(3)
                wait_done(act, U_EXPERT + 23, e * 2)
                fn(YE[:, 0:512], ps[:, 4, :], ACT.Copy).then_inc(ye_a, 1)

            act.wait_ge(x_updated, 8)
            for t in range(TT):
                fn(ZP[:, 2048 + D * t:2048 + D * t + D], X[:, t, :], ACT.Square, scale=D ** -0.5,
                   accum_out=ss[:, t:t + 1]
                   ).then_inc(final_squares, 1)

            with act.Fori(0, NL) as l:
                turns = l * LAYER_TURNS
                vt = turns + U_LAYER // RING

                def vc(key):
                    return lambda c: vcol[:, V2[key] + c:V2[key] + c + 1]

                def ffn(f):
                    def silu(q, done):
                        act.wait_ge(ffn_full, done + (q + 1))
                        fn(FS[:, q % 4, :], ps[:, 4 + q % 4, 0:256], ACT.Silu).then_inc(ffn_silu, 1)

                    done = f * FCH
                    with act.Fori(0, FCH // 4) as b:
                        for q in range(4):
                            silu(q, done + b * 4)
                    for q in range(FCH // 4 * 4, FCH):
                        silu(q, done)

                act.wait_ge(x_updated, l * XL + XB)
                squares(l * 3 + 3, X)
                act.wait_ge(cols_copied, l + 2)
                norm_out(l * 3 + 3, ZT, vc("ffn1"))
                ffn(l * 2)
                act.wait_ge(x_updated, l * XL + (XB + 4))
                squares(l * 3 + 4, X)
                norm_out(l * 3 + 4, ZT, vc("mix"))

                def tile(m, dst, func=ACT.Copy, n=256, parts=TT):
                    wait_done(act, L_TOK + m, vt)
                    fn(dst, ps[:, 4 + m % 4, 0:parts * n].rearrange("p (t n) -> p t n", t=parts), func
                       ).then_inc(tile_out_a, 1)

                na, nv = l * TILES_A + B1_A, l * TILES_V + B1_V
                for m in (0, 2, 4, 6):
                    tile(m, PB[:, :, 256 * m:256 * m + 256])
                act.wait_ge(tile_out_a, na + 4)
                act.wait_ge(tile_out_v, nv + 3)
                fn(SQ2, PB[:, :, 0:NORMED], ACT.Square, scale=HD ** -0.5).then_inc(head_squares, 1)
                for m in (8, 10):
                    tile(m, PB[:, :, 256 * m:256 * m + 256])
                tile(11, PB[:, :, PB_G:PB_G + 24], ACT.Sigmoid, n=24)
                act.wait_ge(head_sums, l + 2)
                tile(13, BX[:, 2:4, :])
                tile(15, YT[:, 1, 2:4, :])

                tile(18, KCV[:])
                tile(19, YT[:, 3, 0:2, :], ACT.Silu)
                tile(20, YT[:, 3, 2:4, :], ACT.Silu)

                tf = l * 9 + 6
                for n, (dst, key) in enumerate(((QT[:, 0:512], "aq"), (QT[:, 1024:1536], "cq"), (QT[:, 2048:2560], "ak"),
                                                (QT[:, 3072:3584], "kw"), (QT[:, 4096:4608], None))):
                    kw = dict(scale=vc(key)(0)) if key else {}
                    turn_copy(dst, tf + (2 * n + 1), 2 * n % 4, **kw)

                wait_done(act, L_CMP + 3, vt)
                act.wait_ge(rope_ready, l + 1)
                fn(GB[:], ps[:, 4:6, 0:256], ACT.Copy).then_inc(cmp_parts, 1)
                act.wait_ge(cmp_summed, l + 1)
                for s in range(2):
                    for hh in range(2):
                        fn(HC[:, s, hh, :], ps[:, 4 + 2 * s + hh, 0:30], ACT.Gelu_apprx_tanh).then_inc(hid_ready, 1)
                wait_done(act, L_CMP + 4, vt)
                fn(KCN[:, 0, :], ps[0:30, 4, 0:HD], ACT.Square, scale=HD ** -0.5, accum_out=kss[0:30, :]).then_inc(kc_squares, 1)

                for t in range(TT):
                    act.wait_ge(ret_full, l * 2 + (t + 1))
                    fn(PB[:, t, PB_DQ:PB_DQ + 512], ps[:, 4 + t, :], ACT.Copy).then_inc(ret_copied, 1)

                ua = l * 12 + 8

                def exps2(sink):
                    def exps(i, unit):
                        b, n = i % 2, P * unit[2]
                        for h in range(4):
                            last = fn(PR[:, b, n * h:n * h + n], PR[:, b, n * h:n * h + n], ACT.Exp,
                                      bias=negmax[:, b, h:h + 1], accum_out=den[:, b, h:h + 1])
                        if sink:
                            last = fn(esink[:, b, :], msink[:, b, :], ACT.Exp)
                        last.then_inc(exp_done, 1)
                    return exps

                units = [(t, 4, t + 1) for t in range(TT) for g in range(2)]
                attention(units, ua, False, exps2(True))
                for n in range(2):
                    y_copy(YT[:, 0, 2 * n:2 * n + 2, :], n, l * 6 + (4 + n + 1))
                act.wait_ge(cmp_shifted, l + 1)
                fn(PCv[:, :, 0:NCMP], PCv[:, :, 0:NCMP], ACT.Exp).then_inc(cmp_exp, 1)
                act.wait_ge(cmp_turned, l + 1)
                fn(PTC, ps[:, 4, :], ACT.Copy).then_inc(cmp_pt, 1)
                attention(units, ua + 4, False, exps2(False))
                attention(units, ua + 8, False, exps2(False))
                act.wait_ge(att_full, ua + 12)
                act.wait_ge(ret_centred, l + 1)
                fn(PR[:, 0, :].rearrange("p (t n) -> p t n", t=TT), PB[:, :, PB_DQ:PB_DQ + 512], ACT.Square,
                   scale=P ** -0.5).then_inc(ret_squares, 1)
                for n in range(2):
                    y_copy(YT[:, 2, 2 * n:2 * n + 2, :], n, l * 6 + (6 + n + 1))

                for i, b in enumerate(BRANCHES):
                    for c in range(KC):
                        q = 8 * i + c
                        if q < EARLY:
                            act.wait_ge(gate_stored, l * EARLY + (q + 1))
                            fn(EG[q], EG[q], ACT.Sigmoid, bias=vc("merge")(KC * b + c)).then_inc(gate_ready, 1)
                            continue
                        if c % 2:
                            wait_done(act, L_GATE + gate_unit(i, c // 2), vt)
                        else:
                            act.wait_ge(gate_even, l * 16 + (q // 2 + 1))
                        act.wait_ge(merged, l * 32 + (q - 1))
                        fn(GB[:, q % 2, :], ps[:, 4 + q % 4, 0:256], ACT.Sigmoid, bias=vc("merge")(KC * b + c)
                           ).then_inc(gate_ready, 1)

                act.wait_ge(x_updated, l * XL + (XB + 8))
                squares(l * 3 + 5, X)
                norm_out(l * 3 + 5, ZT, vc("ffn2"))
                ffn(l * 2 + 1)

        @block.vector
        def _(dve):
            tt, ts, stt = nc.vector.tensor_tensor, nc.vector.tensor_scalar, nc.vector.scalar_tensor_tensor
            copy, reduce = nc.vector.tensor_copy, nc.vector.tensor_reduce
            own = Steps(dve, vsteps)

            def over(ap, n):
                return ap.unsqueeze(2).broadcast_to([ap.shape[0], ap.shape[1], n])

            def over3(ap, n):
                return ap.unsqueeze(3).broadcast_to([*ap.shape, n])

            dve.wait_ge(cols_turned, 1)
            copy(vcol[:, 0:V1_N], ps[:, 0, 0:V1_N]).then_inc(cols_copied, 1)
            dve.wait_ge(c_silu, 1)
            copy(modL[:, :, 0:16], over(cs[:, 0:8], 16)).then_inc(mod_lhs, 1)
            copy(modL[:, :, 16:32], over(cs[:, 8:16], 16)).then_inc(mod_lhs, 1)

            def scaled(v, src):
                dve.wait_ge(norm_rstd, v + 1)
                for t in range(TT):
                    ts(Z[:, t, :], src[:, t, :], rstd[:, t:t + 1], None, ALU.mult).then_inc(norm_scaled, 1)

            def norm_out(v, dst, scale, bias=None):
                for b in (1, 3):
                    dve.wait_ge(norm_turned, v * 4 + (b + 1))
                    for c in (2 * b, 2 * b + 1):
                        src = ps[:, b, 256 * (c % 2):256 * (c % 2) + 256]
                        if bias:
                            ins = ts(dst[:, c, :], src, scale(c), bias(c), ALU.mult, ALU.add)
                        else:
                            ins = ts(dst[:, c, :], src, scale(c), None, ALU.mult)
                        ins.then_inc(norm_out_v, 1)

            scaled(0, X)
            dve.wait_ge(rows_in, 16 * 5)
            with dve.Fori(0, 2) as i:
                dve.wait_ge(modcols_full, i * 4 + 4)
                tt(modcol[:, bass.ds(i * 32, 32)].rearrange("p (c w) -> p c w", w=2),
                   ps[:, 6, 0:32].rearrange("p (c w) -> p c w", w=2),
                   over(vcol[:, bass.ds(i * 24 + V1["b_mod"], 16)], 2), ALU.add).then_inc(modcols_out, 1)
                for r in range(2):
                    dve.wait_ge(modrow_full, i * 2 + (r + 1))
                    row = YF[:, bass.ds(i * D + (2048 + 512 * r), 512)]
                    tt(row, ps[:, 7, :], row, ALU.add).then_inc(modrow_out, 1)

            mc = modcol.rearrange("p (i s c w) -> p i s w c", i=2, s=2, c=8)
            dve.wait_ge(modcols_out, 2)
            for n, (i, w, g) in enumerate(((0, 0, "g_mix"), (0, 1, "g_mix"), (1, 0, "g_ffn"))):
                stt(out=scaleA[:, n, :], in0=mc[:, i, 1, w, :], scalar=1.0, in1=vcol[:, V1[g]:V1[g] + 8],
                    op0=ALU.add, op1=ALU.mult).then_inc(affine_set, 1)
            copy(scaleB[:, 0:2, :], mc[:, 0, 0]).then_inc(affine_set, 1)
            copy(scaleB[:, 2, :], mc[:, 1, 0, 0, :]).then_inc(affine_set, 1)
            dve.wait_ge(affine_set, 5)

            def col(table, i):
                return lambda c: table[:, i, c:c + 1]

            norm_out(0, ZT, col(scaleA, 0), col(scaleB, 0))
            scaled(1, XC)
            norm_out(1, CT, col(scaleA, 1), col(scaleB, 1))

            for m in (1, 3):
                wait_done(dve, U_WIN + (0, 1, 2, 2)[m])
                copy(B1[:, :, 256 * m:256 * m + 256], ps[:, 4 + m, :].rearrange("p (t n) -> p t n", t=TT)
                     ).then_inc(tile_out_v, 1)

            dve.wait_ge(head_squares, 1)
            reduce(hss[:, 0:28], ZP[:, 2048:2048 + TT * 896].rearrange("p (h d) -> p h d", d=HD), AX_X, ALU.add
                   ).then_inc(head_sums, 1)
            dve.wait_ge(head_rstd, 1)
            dve.wait_ge(tile_out_a, 2)
            dve.wait_ge(tile_out_v, 2)
            hr = hrs[:, 0:28].rearrange("p (t h) -> p t h", t=TT)
            qk = B1[:, :, 0:640].rearrange("p t (h d) -> p t h d", d=HD)
            ck = B1[:, :, FB_CK:FB_CK + 128].rearrange("p t (h d) -> p t h d", d=HD)
            own(tt(qk, qk, over3(hr[:, :, 0:10], HD), ALU.mult))
            own(tt(ck, ck, over3(hr[:, :, 12:14], HD), ALU.mult))
            own.settle()

            def gain(g, t, h):
                return g.unsqueeze(1).unsqueeze(1).broadcast_to([P, t, h, HD])

            own(tt(qk[:, :, 0:8], qk[:, :, 0:8], gain(qgain, TT, 8), ALU.mult))
            own(tt(qk[:, :, 8:10], qk[:, :, 8:10], gain(kgain, TT, 2), ALU.mult))
            for t in range(TT):
                own(tt(KN1[:, 2 + t], ck[:, t].unsqueeze(2).broadcast_to([P, 2, 2, HD]), gain(kgain, 2, 2), ALU.mult))
            own.settle()

            def table(name, heads):
                return C(name).rearrange("p (t d) -> p t d", t=TT).unsqueeze(2).broadcast_to([P, TT, heads, 32])

            def rotate(x, name, heads, ta, tb, write):
                for half, (fa, fb, op) in enumerate((("c", "s", ALU.subtract), ("s", "c", ALU.add))):
                    own(tt(ta, x[:, :, :, 0:32], table(name + fa, heads), ALU.mult))
                    own(tt(tb, x[:, :, :, 32:64], table(name + fb, heads), ALU.mult))
                    own.settle()
                    write(half, op)

            def write1(half, op):
                lo, hi = 32 * half, 32 * half + 32
                for t in range(TT):
                    own(tt(KN1[:, t, :, :, lo:hi], RT1[:, 0, t, 8:10].unsqueeze(2).broadcast_to([P, 2, 2, 32]),
                           RT1[:, 1, t, 8:10].unsqueeze(2).broadcast_to([P, 2, 2, 32]), op))
                last = tt(RQ1[:, :, :, lo:hi], RT1[:, 0, :, 0:8], RT1[:, 1, :, 0:8], op)
                if half:
                    last.then_inc(heads_ready, 1)
                else:
                    own(last)
                    own.settle()

            rotate(qk, "rope1", 10, RT1[:, 0], RT1[:, 1], write1)

            def turn_copy(dst, n_full, bank, scale=None):
                dve.wait_ge(turn_full, n_full)
                if scale is None:
                    copy(dst, ps[:, bank, :]).then_inc(turn_out_v, 1)
                else:
                    ts(dst, ps[:, bank, :], scale, None, ALU.mult).then_inc(turn_out_v, 1)

            turn_copy(QT[:, 2560:3072], 2, 1)
            turn_copy(QT[:, 512:1024], 4, 3)
            turn_copy(QT[:, 1536:2048], 6, 1)

            dve.wait_ge(vv_rstd, 1)
            for t in range(TT):
                v = B1[:, t, FB_VV:FB_VV + 512]
                stt(out=v, in0=v, scalar=hrs[:, 28 + t:29 + t], in1=vgain, op0=ALU.mult, op1=ALU.mult
                    ).then_inc(vv_ready, 1)

            def attention(units, base, first, maxima, scale_out):
                def row_maximum(i):
                    dve.wait_ge(scores_full, base + (i + 1))
                    if i >= 2 or not first:
                        dve.wait_ge(exp_done, base + (i - 1))
                        dve.wait_ge(p_turned, base * 2 + 2 * (i - 1))
                    maxima(i, units[i])

                def pt_copy(i):
                    n = units[i][1] * units[i][2] // 2 * P
                    dve.wait_ge(p_turned, base * 2 + (2 * i + 2))
                    copy(PT[:, i % 2, n:2 * n], ps[:, 5, 0:n]).then_inc(pt_out_v, 1)

                row_maximum(0)
                for i in range(len(units)):
                    if i + 1 < len(units):
                        row_maximum(i + 1)
                    pt_copy(i)
                    dve.wait_ge(exp_done, base + (i + 1))
                    scale_out(i, units[i])

            def maxima1(i, unit):
                b = i % 2
                own(reduce(negmax[:, b, 0:2], ps[:, 2 * b:2 * b + 2, :], AX_X, ALU.max))
                own.settle()
                ts(negmax[:, b, 0:2], negmax[:, b, 0:2], -SCALE, None, ALU.mult).then_inc(row_max, 1)

            def scale1(i, unit):
                t, _, _, hp = unit
                b = i % 2
                own(nc.vector.reciprocal(rden[:, b, 0:2], den[:, b, 0:2]))
                own.settle()
                dve.wait_ge(att_full, i + 1)
                tt(B1[:, t, P * hp:P * hp + P].rearrange("p (h d) -> p h d", h=2),
                   ps[:, 6 + b, 0:P].rearrange("p (h d) -> p h d", h=2), over(rden[:, b, 0:2], HD), ALU.mult
                   ).then_inc(att_scaled, 1)

            attention([(t, 2, 4, hp) for t in range(TT) for hp in range(4)], 0, True, maxima1, scale1)

            for t in range(TT):
                dve.wait_ge(gm_full, t + 1)
                if t:
                    dve.wait_ge(gm_out, t)
                u = B1[:, t, FB_U:FB_U + 512]
                own(tt(vgain.rearrange("p (g d) -> p g d", g=8), ps[:, t, :].rearrange("p (g d) -> p g d", g=8),
                       over(vcol[:, V1["b_s"]:V1["b_s"] + 8], HD), ALU.add))
                own.settle()
                tt(u, u, vgain, ALU.mult).then_inc(gm_out, 1)

            def gated_update(i, bank0):
                for b in range(4):
                    own(tt(PG[b], ps[:, bank0 + b, :], GT[:, i, 512 * (b % 2):512 * (b % 2) + 512], ALU.mult))
                own.settle()
                for b in range(4):
                    x = X[:, b // 2, 512 * (b % 2):512 * (b % 2) + 512]
                    tt(x, x, PG[b], ALU.add).then_inc(x_updated, 1)

            wait_done(dve, U_WOUT + 3)
            gated_update(0, 4)
            dve.wait_ge(x_updated, 4)
            scaled(2, X)
            norm_out(2, ZT, col(scaleA, 2), col(scaleB, 2))

            wait_done(dve, U_ROUTER)
            for t in range(TT):
                reduce(hrs[:, t:t + 1], ps[:, 4, NE * t:NE * t + NE], AX_X, ALU.max, negate=True).then_inc(aff_max, 1)
            dve.wait_ge(aff_exp, 2)
            own(nc.vector.reciprocal(hrs[:, 2:4], lsum[:, 2:4]))
            own.settle()
            own(ts(AFF[:, 0, :], AFF[:, 0, :], hrs[:, 2:3], None, ALU.mult))
            ts(AFF[:, 1, :], AFF[:, 1, :], hrs[:, 3:4], None, ALU.mult).then_inc(aff_ready, 1)

            dve.wait_ge(afft_full, 1)
            own(copy(WORK, ps[0:NE, 5, 0:T]))
            for r in range(CAP // 8):
                own.settle()
                own(nc.vector.max(VALS[:, 8 * r:8 * r + 8], WORK))
                own.settle()
                own(nc.vector.max_index(IDX[:, 8 * r:8 * r + 8], VALS[:, 8 * r:8 * r + 8], WORK))
                own.settle()
                if r < CAP // 8 - 1:
                    own(nc.vector.match_replace(WORK, VALS[:, 8 * r:8 * r + 8], WORK, -1.0))
            for rep, src in ((REPI, IDX), (REPV, VALS)):
                copy(rep.rearrange("e (j s) -> e j s", j=4), src.unsqueeze(1).broadcast_to([NE, 4, CAP])
                     ).then_inc(top_ready, 1)
            dve.wait_ge(slots_full, 1)
            own(copy(small[:, 322:354], ps[:, 6, 0:2 * NE]))
            own.settle()

            with dve.Fori(0, NE) as e:
                own.loop(e, NE, 1)
                dve.wait_ge(sel_turned, e)
                ts(SEL, C("iota"), idxcol[:, bass.ds(e, 1)], None, ALU.is_equal).then_inc(sel_ready, 1)
                dve.wait_ge(scattered, e)
                ts(SELG, C("iota"), idxcol[:, bass.ds(e, 1)], gatecol[:, bass.ds(e, 1)], ALU.is_equal, ALU.mult
                   ).then_inc(sel_ready, 1)
                dve.wait_ge(sel_turned, e + 1)
                copy(OH, ps[:, 4, 0:2 * P].rearrange("p (t s) -> p t s", t=TT)[:, :, 0:CAP]).then_inc(oh_ready, 1)
                dve.wait_ge(xe_full, e + 1)
                own(tt(XE, ps[:, 5, 0:256].rearrange("p (k s) -> p k s", k=KC), over(scaleA[:, 2, :], CAP), ALU.mult))
                own.settle()
                tt(XE, XE, over(scaleB[:, 2, :], CAP), ALU.add).then_inc(xe_ready, 1)

                def part_copy(ch):
                    wait_done(dve, U_EXPERT + 4 * ch + 3, e * 2)
                    copy(PG[2 + ch % 2], ps[:, 5, :]).then_inc(pu_copied, 1)

                def hidden(ch):
                    dve.wait_ge(sg_ready, e * 4 + (ch + 1))
                    tt(HT[:, 4 * ch:4 * ch + 4, :].rearrange("p f s -> p (f s)"), SG, ps[:, 6 + ch % 2, P:2 * P],
                       ALU.mult).then_inc(ht_ready, 1)

                for ch in range(4):
                    part_copy(ch)
                    if ch:
                        hidden(ch - 1)
                hidden(3)
                wait_done(dve, U_EXPERT + 23, e * 2)
                copy(YE[:, 512:1024], ps[:, 5, :]).then_inc(ye_v, 1)
            own.end()

            dve.wait_ge(moe_full, 1)
            gated_update(1, 0)
            dve.wait_ge(final_rstd, 1)
            dve.wait_ge(gfinal_in, 16)
            for t in range(TT):
                stt(out=X[:, t, :], in0=X[:, t, :], scalar=rstd[:, t:t + 1], in1=gfinal, op0=ALU.mult, op1=ALU.mult
                    ).then_inc(x_updated, 1)

            with dve.Fori(0, NL) as l:
                own.loop(l, NL, OWN_V)
                turns = l * LAYER_TURNS
                vt = turns + U_LAYER // RING

                def vc(key, c=0):
                    return vcol[:, V2[key] + c:V2[key] + c + 1]

                def vcf(key):
                    return lambda c: vc(key, c)

                dve.wait_ge(cols_turned, l + 2)
                copy(vcol[:, 0:V2_N], ps[:, 7, 0:V2_N]).then_inc(cols_copied, 1)
                dve.wait_ge(v2_in, l * 16 * V2_LOADS + 16 * V2_LOADS)
                own(ts(nsinks, sinks, -1.0, None, ALU.mult))
                dve.wait_ge(cols_copied, l + 2)

                def ffn(f, last_unit, update):
                    def hidden(q, done):
                        dve.wait_ge(ffn_silu, done + (q + 1))
                        tt(FH[:, q % 4, :], FS[:, q % 4, :], ps[:, 4 + q % 4, 256:512], ALU.mult).then_inc(ffn_hidden, 1)

                    done = f * FCH
                    with dve.Fori(0, FCH // 4) as b:
                        for q in range(4):
                            hidden(q, done + b * 4)
                    for q in range(FCH // 4 * 4, FCH):
                        hidden(q, done)
                    wait_done(dve, last_unit, vt)
                    for t in range(TT):
                        for half in range(2):
                            x = X[:, t, 512 * half:512 * half + 512]
                            stt(out=x, in0=ps[:, 2 * t + half, :], scalar=0.5, in1=x, op0=ALU.mult, op1=ALU.add
                                ).then_inc(x_updated, 1)
                    dve.wait_ge(x_updated, update)

                scaled(l * 3 + 3, X)
                norm_out(l * 3 + 3, ZT, vcf("ffn1"))
                ffn(l * 2, L_FFN1 + 32, l * XL + (XB + 4))
                scaled(l * 3 + 4, X)
                norm_out(l * 3 + 4, ZT, vcf("mix"))

                def bank(m, n=256, parts=TT):
                    wait_done(dve, L_TOK + m, vt)
                    return ps[:, 4 + m % 4, 0:parts * n].rearrange("p (t n) -> p t n", t=parts)

                na, nv = l * TILES_A + B1_A, l * TILES_V + B1_V
                for m in (1, 3, 5, 7, 9):
                    copy(PB[:, :, 256 * m:256 * m + 256], bank(m)).then_inc(tile_out_v, 1)
                    if m == 7:
                        dve.wait_ge(head_squares, l + 2)
                        reduce(hss[:, 0:52], ZP[:, 0:TT * NORMED].rearrange("p (h d) -> p h d", d=HD), AX_X, ALU.add
                               ).then_inc(head_sums, 1)

                dve.wait_ge(head_rstd, l + 2)
                dve.wait_ge(tile_out_a, na + 4)
                dve.wait_ge(tile_out_v, nv + 5)
                hr = hrs[:, 0:52].rearrange("p (t h) -> p t h", t=TT)
                for c0 in (PB_AQ, PB_CQ):
                    x = PB[:, :, c0:c0 + 512].rearrange("p t (h d) -> p t h d", d=HD)
                    own(tt(x, x, over3(hr[:, :, c0 // HD:c0 // HD + 8], HD), ALU.mult))
                for k, c0 in enumerate((PB_AK, PB_KS, PB_KW)):
                    for t in range(TT):
                        x = PB[:, t, c0:c0 + P].rearrange("p (g d) -> p g d", g=2).unsqueeze(2)
                        r = hr[:, t, c0 // HD:c0 // HD + 2].unsqueeze(2).unsqueeze(3)
                        last = tt(KN[:, t, k], x.broadcast_to([P, 2, 2, HD]), r.broadcast_to([P, 2, 2, HD]), ALU.mult)
                        if k == 2 and t == 1:
                            last.then_inc(heads_ready, 1)
                        else:
                            own(last)

                def write2(half, op):
                    last = tt(RQ[:, :, :, 32 * half:32 * half + 32], RTa, RTb, op)
                    if half:
                        last.then_inc(rope_ready, 1)
                    else:
                        own(last)
                        own.settle()

                wait_tile(dve, 8, TILE_BY, na, nv)
                rotate(PB[:, :, PB_DQ:PB_DQ + 512].rearrange("p t (h d) -> p t h d", d=HD), "rope2", 8, RTa, RTb, write2)

                copy(BX[:, 0:2, :], bank(12)).then_inc(tile_out_v, 1)
                copy(YT[:, 1, 0:2, :], bank(14)).then_inc(tile_out_v, 1)
                own(nc.vector.memset(ZC[:, :, 0:2], 0.0))
                dve.wait_ge(tile_out_v, nv + 7)
                tt(ZC[:, 0:2, 2:258], bank(16), BX[:, 0:2, :], ALU.mult).then_inc(tile_out_v, 1)
                wait_tile(dve, 13, TILE_BY, na, nv)
                tt(ZC[:, 2:4, 2:258], bank(17), BX[:, 2:4, :], ALU.mult).then_inc(tile_out_v, 1)
                own.settle()
                dve.wait_ge(tile_out_v, nv + 9)
                for c in range(4):
                    own(ts(BX[:, c, :], ZC[:, c, 2:258], vc("conv", 8 + c), None, ALU.mult))
                for k in (1, 0):
                    own.settle()
                    for c in range(4):
                        own(stt(out=BX[:, c, :], in0=ZC[:, c, k:k + 256], scalar=vc("conv", 4 * k + c), in1=BX[:, c, :],
                                op0=ALU.mult, op1=ALU.add))
                own.settle()
                wait_tile(dve, 15, TILE_BY, na, nv)
                for c in range(4):
                    tt(YT[:, 1, c, :], YT[:, 1, c, :], BX[:, c, :], ALU.mult).then_inc(conv_ready, 1)

                wait_tile(dve, 18, TILE_BY, na, nv)
                for lh in range(2):
                    last = tt(BLK[:, 16 * lh:16 * lh + 16],
                              KCV[:, :, 16 * lh:16 * lh + 16 * NCMP].rearrange("p g (n l) -> p l g n", l=16),
                              over3(over(vcol[:, V2["pos"] + 16 * lh:V2["pos"] + 16 * lh + 16], 2), NCMP), ALU.add)
                    own(last) if lh == 0 else last.then_inc(blk_ready, 1)

                tf = l * 9 + 6
                for n, (dst, scale) in enumerate(((QT[:, 512:1024], vc("aq")), (QT[:, 1536:2048], vc("cq")),
                                                  (QT[:, 2560:3072], vc("ks")), (QT[:, 3584:4096], None))):
                    turn_copy(dst, tf + (2 * n + 2), (2 * n + 1) % 4, scale)

                wait_done(dve, L_CMP + 4, vt)
                dve.wait_ge(cmp_cleared, l + 1)
                for h in range(4):
                    last = copy(VB[32 * h:32 * h + NCMP, HD * h:HD * h + HD], ps[0:NCMP, 5, HD * (h // 2):HD * (h // 2) + HD])
                    own(last) if h < 3 else last.then_inc(vb_ready, 1)
                dve.wait_ge(kc_rstd, l + 1)
                ts(KCN, ps[0:30, 4, 0:HD].unsqueeze(1).broadcast_to([30, 2, HD]), krs[0:30, :], None, ALU.mult
                   ).then_inc(kcn_ready, 1)
                dve.wait_ge(kct_full, l + 1)
                ts(kcT, ps[:, 6, 0:30], vc("kc"), None, ALU.mult).then_inc(kct_out, 1)

                for i, d in enumerate(("decay0", "decay1", "decay0")):
                    dve.wait_ge(ret_scores, l * 2 + (i // 2 + 1))
                    for r in range(2):
                        tt(AT[:, i, :].rearrange("p (h r n) -> p r h n", r=2, h=2)[:, r],
                           C(d).rearrange("p (h r n) -> p r h n", r=2, h=2)[:, r],
                           ps[:, 2 * (i // 2) + r, 256 * (i % 2):256 * (i % 2) + 256].rearrange("p (h n) -> p h n", h=2),
                           ALU.mult).then_inc(ret_decayed, 1)
                dve.wait_ge(ret_copied, l * 2 + 2)
                ro = PB[:, :, PB_DQ:PB_DQ + 512].rearrange("p t (h d) -> p t h d", d=P)
                own(reduce(gmean, ro, AX_X, ALU.add))
                own.settle()
                own(ts(gmean, gmean, -1.0 / P, None, ALU.mult))
                own.settle()
                tt(ro, ro, over3(gmean.rearrange("p (t h) -> p t h", t=TT), P), ALU.add).then_inc(ret_centred, 1)

                ua = l * 12 + 8

                def paired(ap):
                    return ap.rearrange("p (h r) -> p r h", r=2)

                def order(ap):
                    return ap.rearrange("p (r h) -> p r h", r=2)

                def maxima2(masks, sink):
                    def maxima(i, unit):
                        b, t, n, g = i % 2, unit[0], P * unit[2], unit[3]
                        pr = PR[:, b, 0:4 * n].rearrange("p (h n) -> p h n", h=4)
                        sc = ps[:, 2 * b:2 * b + 2, :].rearrange("p b (h n) -> p (b h) n", h=2)[:, :, 0:n]
                        own(stt(out=pr, in0=sc, scalar=SCALE,
                                in1=C(masks[t]).unsqueeze(1).broadcast_to([P, 4, n]), op0=ALU.mult, op1=ALU.add))
                        own.settle()
                        last = reduce(negmax[:, b, :], pr, AX_X, ALU.max, negate=True)
                        if sink:
                            own(last)
                            own.settle()
                            own(tt(order(negmax[:, b, :]), order(negmax[:, b, :]), paired(nsinks[:, 4 * g:4 * g + 4]), ALU.min))
                            own.settle()
                            last = tt(order(msink[:, b, :]), paired(sinks[:, 4 * g:4 * g + 4]), order(negmax[:, b, :]), ALU.add)
                        last.then_inc(row_max, 1)
                    return maxima

                def store_gate(q):
                    copy(EG[q], ps[:, 6 + q % 2, 256:512]).then_inc(gate_stored, 1)

                def scale2(base, dst, gate, early):
                    def scale_out(i, unit):
                        t, g, b = unit[0], unit[3], i % 2
                        if gate is None:
                            own(tt(den[:, b, :], den[:, b, :], esink[:, b, :], ALU.add))
                            own.settle()
                        own(ts(den[:, b, :], den[:, b, :], TINY, None, ALU.max))
                        own.settle()
                        own(nc.vector.reciprocal(rden[:, b, :], den[:, b, :]))
                        own.settle()
                        if gate is not None:
                            c0 = PB_G + 12 * g
                            own(tt(order(rden[:, b, :]), order(rden[:, b, :]),
                                   PB[:, t, c0:c0 + 12].rearrange("p (h r j) -> p j r h", j=3, r=2)[:, gate], ALU.mult))
                            own.settle()
                        dve.wait_ge(att_full, base + (i + 1))
                        o = PB[:, t, dst + 256 * g:dst + 256 * g + 256].rearrange("p (h r d) -> p r h d", h=2, r=2)
                        sc = ps[:, 6 + b, 0:256].rearrange("p (r h d) -> p r h d", h=2, r=2)
                        w = over3(order(rden[:, b, :]), HD)
                        if gate is None:
                            tt(o, sc, w, ALU.mult).then_inc(att_scaled, 1)
                            store_gate(early + i)
                        else:
                            tmp = GBf[:, 0:256].rearrange("p (r h d) -> p r h d", h=2, r=2)
                            dve.wait_ge(att_scaled, base + i)
                            own(tt(tmp, sc, w, ALU.mult))
                            store_gate(early + i)
                            own.settle()
                            tt(o, o, tmp, ALU.add).then_inc(att_scaled, 1)
                    return scale_out

                units = [(t, 4, t + 1, g) for t in range(TT) for g in range(2)]
                attention(units, ua, False, maxima2(("causal0", "window1"), True), scale2(ua, PB_AQ, None, 0))

                dve.wait_ge(cmp_scores, l + 1)
                pc = PCv[:, :, 0:NCMP]
                for r in range(2):
                    own(stt(out=pc[:, 8 * r:8 * r + 8], in0=ps[:, r, 0:256].rearrange("p (h n) -> p h n", h=8)[:, :, 0:NCMP],
                            scalar=SCALE, in1=C("cmp").rearrange("p (h n) -> p h n", h=8), op0=ALU.mult, op1=ALU.add))
                own.settle()
                own(reduce(cneg, pc, AX_X, ALU.max, negate=True))
                own.settle()
                own(ts(cneg, cneg, FLOOR, None, ALU.min))
                own.settle()
                tt(pc, pc, over(cneg, NCMP), ALU.add).then_inc(cmp_shifted, 1)
                dve.wait_ge(cmp_exp, l + 1)
                own(reduce(cden, pc, AX_X, ALU.add))
                own.settle()
                own(ts(cden, cden, TINY, None, ALU.max))
                own.settle()
                own(nc.vector.reciprocal(cneg, cden))
                own.settle()
                own(tt(cden.rearrange("p (r t h) -> p r t h", t=TT, r=2), cneg.rearrange("p (r t h) -> p r t h", t=TT, r=2),
                       PB[:, :, PB_G:PB_G + 24].rearrange("p t (h r j) -> p j r t h", j=3, r=2)[:, 0], ALU.mult))
                own.settle()
                dve.wait_ge(cmp_full, l + 1)
                for t in range(TT):
                    tt(PB[:, t, PB_CQ:PB_CQ + 512].rearrange("p (h r d) -> p r h d", h=4, r=2),
                       ps[:, 6 + t, :].rearrange("p (r h d) -> p r h d", h=4, r=2),
                       over3(cden.rearrange("p (r t h) -> p t r h", t=TT, r=2)[:, t], HD), ALU.mult).then_inc(cmp_out, 1)
                dve.wait_ge(cmp_out, l * 2 + 2)

                attention(units, ua + 4, False, maxima2(("causal0", "causal1"), False), scale2(ua + 4, PB_CQ, 1, 4))
                dve.wait_ge(att_scaled, ua + 8)
                attention(units, ua + 8, False, maxima2(("causal0", "causal1"), False), scale2(ua + 8, PB_CQ, 2, 8))

                dve.wait_ge(ret_squares, l + 1)
                reduce(gmean, PR[:, 0, :].rearrange("p (h d) -> p h d", d=P), AX_X, ALU.add).then_inc(ret_sums, 1)
                dve.wait_ge(ret_rstd, l + 1)
                tt(ro, ro, over3(hrs[:, 0:8].rearrange("p (t h) -> p t h", t=TT), P), ALU.mult).then_inc(ret_normed, 1)
                for n in range(2):
                    dve.wait_ge(y_full, l * 6 + (8 + n + 1))
                    for c in range(2):
                        y = YT[:, 3, 2 * n + c, :]
                        last = stt(out=y, in0=ps[:, 2 + n, 256 * c:256 * c + 256], scalar=vc("ret", 2 * n + c), in1=y,
                                   op0=ALU.mult, op1=ALU.mult)
                        last.then_inc(yd_out, 1) if c else own(last)

                for i in range(4):
                    for c in range(KC):
                        q = 8 * i + c
                        dve.wait_ge(gate_ready, l * 32 + (q + 1))
                        if q == KC - 1:
                            wait_done(dve, L_GATE + branch_unit(0) + 1, vt)
                        elif q < EARLY:
                            dve.wait_ge(branch_full, l * (EARLY - 1) + (q + 1 if q < KC else q))
                        g = EG[q] if q < EARLY else GB[:, q % 2, :]
                        y = ps[:, 4 + q % 4, 256:512]
                        if i == 0:
                            tt(MT[:, c, :], g, y, ALU.mult).then_inc(merged, 1)
                        else:
                            tmp = ZP[:, 2048 + 256 * (q % 2):2304 + 256 * (q % 2)]
                            dve.wait_ge(merged, l * 32 + (q - 1))
                            own(tt(tmp, g, y, ALU.mult))
                            own.settle()
                            tt(MT[:, c, :], MT[:, c, :], tmp, ALU.add).then_inc(merged, 1)
                wait_done(dve, L_OUT + 3, vt)
                for t in range(TT):
                    for half in range(2):
                        x = X[:, t, 512 * half:512 * half + 512]
                        tt(x, x, ps[:, 4 + 2 * t + half, :], ALU.add).then_inc(x_updated, 1)
                dve.wait_ge(x_updated, l * XL + (XB + 8))
                scaled(l * 3 + 5, X)
                norm_out(l * 3 + 5, ZT, vcf("ffn2"))
                ffn(l * 2 + 1, L_FFN2 + 32, l * XL + (XB + 12))
            own.end()

        @block.gpsimd
        def _(pool):
            own = Steps(pool, psteps)
            own(nc.gpsimd.memset(power, -0.5))
            own(nc.gpsimd.memset(eps, EPS))
            own.settle()

            def root(dst, mean, done, parts=P):
                own(nc.gpsimd.tensor_tensor(dst, mean, eps[0:parts, :].broadcast_to([parts, dst.shape[1]]), ALU.add))
                own.settle()
                nc.gpsimd.tensor_tensor(dst, dst, power[0:parts, :].broadcast_to([parts, dst.shape[1]]), ALU.pow
                                        ).then_inc(done, 1)

            def norm(v):
                pool.wait_ge(norm_squares, v * 2 + 2)
                root(rstd, ss, norm_rstd)

            norm(0)
            norm(1)
            pool.wait_ge(head_sums, 1)
            root(hrs[:, 0:28], hss[:, 0:28], head_rstd)
            pool.wait_ge(vv_squares, 2)
            root(hrs[:, 28:30], lsum[:, 0:2], vv_rstd)
            norm(2)
            nc.gpsimd.memset(zeros, 0.0).then_inc(zeros_set, 1)
            pool.wait_ge(final_squares, 2)
            root(rstd, ss, final_rstd)
            with pool.Fori(0, NL) as l:
                own.loop(l, NL, 6)
                norm(l * 3 + 3)
                norm(l * 3 + 4)
                nc.gpsimd.memset(YF[:, 2048:3072], 0.0).then_inc(cmp_cleared, 1)
                pool.wait_ge(head_sums, l + 2)
                root(hrs[:, 0:52], hss[:, 0:52], head_rstd)
                pool.wait_ge(kc_squares, l + 1)
                root(krs[0:30, :], kss[0:30, :], kc_rstd, 30)
                pool.wait_ge(ret_sums, l + 1)
                root(hrs[:, 0:8], gmean, ret_rstd)
                norm(l * 3 + 5)
            own.end()
        return nc


_INS = ['x', 'c', 'ctx', 'c_ctx', 'w_mod', 'b_mod', 'g_mix', 'g_ffn', 'w_in', 'q_gain', 'k_gain', 'v_gain', 'w_s', 'b_s',
        'w_out', 'w_router', 'w1', 'w3', 'w2', 'g_final', 'ffn1_norm_2', 'ffn1_w_gate_2', 'ffn1_w_up_2',
        'ffn1_w_down_2', 'mix_norm_2', 'w_in_2', 'merge_gate_bias_2', 'swa_q_gain_2', 'swa_k_gain_2', 'swa_sinks_2',
        'conv_w_2', 'nsa_q_gain_2', 'nsa_k_gain_2', 'cmp_pos_k_2', 'cmp_pos_v_2', 'cmp_wk1_2', 'cmp_wk2_2',
        'cmp_wv1_2', 'cmp_wv2_2', 'ret_norm_gain_2', 'w_branch_2', 'w_out_2', 'ffn2_norm_2', 'ffn2_w_gate_2',
        'ffn2_w_up_2', 'ffn2_w_down_2']


def kernel(**inputs):
    import concourse.bacc as _bacc
    from concourse.bass_utils import run_bass_kernel_spmd as _run

    nc = _bacc.Bacc("TRN2", target_bir_lowering=False, num_devices=1)
    arrays, args = {}, {}
    for name in _INS:
        arr = np.ascontiguousarray(inputs[name])
        arrays[f"in_{name}"] = arr
        args[name] = nc.dram_tensor(f"in_{name}", arr.shape, mybir.dt.from_np(arr.dtype), kind="ExternalInput").ap()
    table, at = const_table()
    arrays["in_constants"] = table
    const = nc.dram_tensor("in_constants", table.shape, F32, kind="ExternalInput").ap()
    out = nc.dram_tensor("out_0", (1, T, D), F32, kind="ExternalOutput").ap()
    build(nc, args, out, const, at)
    r = _run(nc, [arrays], core_ids=[0])
    return r.results[0]["out_0"]
```
